# Optimizing a Trainium2 kernel written in Bass

```python
import math
import jax, jax.numpy as jnp
from jax import lax
import numpy as np

D_MODEL = 1024
BATCH = 1
SEQ = 512
DEPTH = 1

CHUNK = 64
D_MIX = D_MODEL
D_SSM = D_MIX // 2
D_ATT = D_MIX - D_SSM
SSM_GROUP = 16
N_SSM_GROUPS = D_SSM // SSM_GROUP
SSM_STATE = 64
HEAD_DIM = 64
N_HEADS = D_ATT // HEAD_DIM
LEFT_CHUNKS = 8
BAND = (LEFT_CHUNKS + 1) * CHUNK
MAX_REL = 128
D_FF = -(-8 * D_MODEL // (3 * 256)) * 256
D_IN = D_SSM + 3 * D_ATT
EPS = 1e-6
DT_MIN = 1e-3
DT_MAX = 1e-1


def rmsnorm(x, g):
    xf = x.astype(jnp.float32)
    y = xf * lax.rsqrt(jnp.mean(xf * xf, axis=-1, keepdims=True) + EPS)
    return (y * g.astype(jnp.float32)).astype(x.dtype)

def s5_mixer(u, lam_re, lam_im, log_dt, b_re, b_im, c_re, c_im, d_skip, w_glu, b_glu):
    bsz, seq, _ = u.shape
    f32 = jnp.float32
    uf = u.astype(f32).reshape(bsz, seq, N_SSM_GROUPS, SSM_GROUP)
    lam = lax.complex(lam_re.astype(f32), lam_im.astype(f32))
    dt = jnp.exp(log_dt.astype(f32))[:, None]
    lam_bar = jnp.exp(lam * dt)
    b_mat = lax.complex(b_re.astype(f32), b_im.astype(f32))
    b_bar = ((lam_bar - 1.0) / lam)[..., None] * b_mat
    bu = jnp.einsum('bsgh,gph->bsgp', uf.astype(jnp.complex64), b_bar)
    a = jnp.broadcast_to(lam_bar, bu.shape)

    def combine(left, right):
        a_l, b_l = left
        a_r, b_r = right
        return a_r * a_l, a_r * b_l + b_r

    _, states = lax.associative_scan(combine, (a, bu), axis=1)
    c_mat = lax.complex(c_re.astype(f32), c_im.astype(f32))
    y = jnp.einsum('bsgp,ghp->bsgh', states, c_mat).real + d_skip.astype(f32) * uf
    y = jax.nn.gelu(y.reshape(bsz, seq, D_SSM))
    y = y * jax.nn.sigmoid(y @ w_glu.astype(f32) + b_glu.astype(f32))
    return y.astype(u.dtype)

def chunked_attention(q, k, v, rel_bias):
    bsz, seq, _ = q.shape
    n_chunks = seq // CHUNK
    shp = (bsz, n_chunks, CHUNK, N_HEADS, HEAD_DIM)
    qc, kc, vc = q.reshape(shp), k.reshape(shp), v.reshape(shp)
    pad = ((0, 0), (LEFT_CHUNKS, 0), (0, 0), (0, 0), (0, 0))
    kp, vp = jnp.pad(kc, pad), jnp.pad(vc, pad)
    kb = jnp.concatenate([kp[:, j:j + n_chunks] for j in range(LEFT_CHUNKS + 1)], axis=2)
    vb = jnp.concatenate([vp[:, j:j + n_chunks] for j in range(LEFT_CHUNKS + 1)], axis=2)
    key_chunk = jnp.arange(n_chunks)[:, None] - LEFT_CHUNKS + (jnp.arange(BAND) // CHUNK)[None, :]
    valid = key_chunk >= 0
    rel = jnp.arange(BAND)[None, :] - LEFT_CHUNKS * CHUNK - jnp.arange(CHUNK)[:, None]
    idx = jnp.clip(rel, -MAX_REL, MAX_REL) + MAX_REL
    bias = rel_bias.astype(jnp.float32)[:, idx]
    scores = jnp.einsum('bnqhd,bnkhd->bhnqk', qc, kb).astype(jnp.float32) / math.sqrt(HEAD_DIM)
    scores = scores + bias[None, :, None, :, :]
    scores = jnp.where(valid[None, None, :, None, :], scores, -1e30)
    probs = jax.nn.softmax(scores, axis=-1)
    out = jnp.einsum('bhnqk,bnkhd->bnqhd', probs.astype(v.dtype), vb)
    return out.reshape(bsz, seq, D_ATT)

def first_inputs(seed: int = 0) -> dict:
    key = jax.random.key(seed)
    ks = jax.random.split(key, 24)
    f32 = jnp.float32
    L, G, P, H = DEPTH, N_SSM_GROUPS, SSM_STATE, SSM_GROUP

    def nrm(k, shape, scale):
        return jax.random.normal(k, shape, f32) * scale

    def gain(k, n):
        return 1.0 + 0.05 * jax.random.normal(k, (L, n), f32)

    lam_re = -0.5 + 0.01 * jax.random.normal(ks[3], (L, G, P), f32)
    lam_im = math.pi * jnp.arange(P, dtype=f32)[None, None, :] + 0.01 * jax.random.normal(ks[4], (L, G, P), f32)
    log_dt = jax.random.uniform(ks[5], (L, G), f32, math.log(DT_MIN), math.log(DT_MAX))
    return {
        "x": jax.random.normal(ks[0], (BATCH, SEQ, D_MODEL), f32),
        "norm_mix_g": gain(ks[1], D_MODEL),
        "w_in": nrm(ks[2], (L, D_MODEL, D_IN), D_MODEL ** -0.5),
        "ssm_lam_re": lam_re,
        "ssm_lam_im": lam_im,
        "ssm_log_dt": log_dt,
        "ssm_b_re": nrm(ks[6], (L, G, P, H), (2.0 * H) ** -0.5),
        "ssm_b_im": nrm(ks[7], (L, G, P, H), (2.0 * H) ** -0.5),
        "ssm_c_re": nrm(ks[8], (L, G, H, P), (2.0 * P) ** -0.5),
        "ssm_c_im": nrm(ks[9], (L, G, H, P), (2.0 * P) ** -0.5),
        "ssm_d": nrm(ks[10], (L, G, H), 1.0),
        "ssm_w_glu": nrm(ks[11], (L, D_SSM, D_SSM), D_SSM ** -0.5),
        "ssm_b_glu": nrm(ks[12], (L, D_SSM), 0.02),
        "attn_rel_bias": nrm(ks[13], (L, N_HEADS, 2 * MAX_REL + 1), 0.5),
        "norm_ssm_out_g": gain(ks[14], D_SSM),
        "norm_att_out_g": gain(ks[15], D_ATT),
        "w_out": nrm(ks[16], (L, D_MIX, D_MODEL), D_MIX ** -0.5),
        "norm_ffn_g": gain(ks[17], D_MODEL),
        "w_gate": nrm(ks[18], (L, D_MODEL, D_FF), D_MODEL ** -0.5),
        "w_up": nrm(ks[19], (L, D_MODEL, D_FF), D_MODEL ** -0.5),
        "w_down": nrm(ks[20], (L, D_FF, D_MODEL), D_FF ** -0.5),
        "norm_final_g": 1.0 + 0.05 * jax.random.normal(ks[21], (D_MODEL,), f32),
    }

def first_block(x, norm_mix_g, w_in, ssm_lam_re, ssm_lam_im, ssm_log_dt, ssm_b_re, ssm_b_im,
              ssm_c_re, ssm_c_im, ssm_d, ssm_w_glu, ssm_b_glu, attn_rel_bias,
              norm_ssm_out_g, norm_att_out_g, w_out, norm_ffn_g, w_gate, w_up, w_down,
              norm_final_g):
    for l in range(DEPTH):
        h = rmsnorm(x, norm_mix_g[l])
        proj = h @ w_in[l]
        u_ssm = proj[..., :D_SSM]
        q = proj[..., D_SSM:D_SSM + D_ATT]
        k = proj[..., D_SSM + D_ATT:D_SSM + 2 * D_ATT]
        v = proj[..., D_SSM + 2 * D_ATT:]
        y_ssm = s5_mixer(u_ssm, ssm_lam_re[l], ssm_lam_im[l], ssm_log_dt[l], ssm_b_re[l], ssm_b_im[l],
                         ssm_c_re[l], ssm_c_im[l], ssm_d[l], ssm_w_glu[l], ssm_b_glu[l])
        y_att = chunked_attention(q, k, v, attn_rel_bias[l])
        mixed = jnp.concatenate([rmsnorm(y_ssm, norm_ssm_out_g[l]),
                                 rmsnorm(y_att, norm_att_out_g[l])], axis=-1)
        x = x + mixed @ w_out[l]
        h2 = rmsnorm(x, norm_ffn_g[l])
        x = x + (jax.nn.silu(h2 @ w_gate[l]) * (h2 @ w_up[l])) @ w_down[l]
    return rmsnorm(x, norm_final_g)


DEPTH_2 = 4

N_MIXERS = 3
SB_HEAD_DIM = 128
SB_HEADS = D_MODEL // SB_HEAD_DIM
DIFF_HALF_DIM = 128
DIFF_HEADS = D_MODEL // (2 * DIFF_HALF_DIM)
MEM_HEAD_DIM = 64
MEM_HEADS = 4
MEM_LEN = 256
MEM_WIDTH = MEM_HEADS * MEM_HEAD_DIM
MIX_WIDTH = D_MODEL
IN_WIDTH = 3 * MIX_WIDTH + MEM_WIDTH
OUT_IN_WIDTH = MIX_WIDTH + MEM_WIDTH
CONV_WIDTH = 3
D_FF_2 = -(-8 * D_MODEL // (3 * 256)) * 256
BLOCK_Q = 128
N_DIFF = (DEPTH_2 + 1) // 3
N_CONV = DEPTH_2 // 3
NORM_EPS = 1e-6
HEAD_NORM_EPS = 1e-5
LAMBDA_STD = 0.1


def _rmsnorm(x, g, eps=NORM_EPS):
    xf = x.astype(jnp.float32)
    y = xf * lax.rsqrt(jnp.mean(xf * xf, axis=-1, keepdims=True) + eps)
    return (y * g.astype(jnp.float32)).astype(x.dtype)

def _heads(t, n_heads, d):
    b, s, _ = t.shape
    return t.reshape(b, s, n_heads, d).transpose(0, 2, 1, 3)

def _rev_cumsum(u):
    shp = u.shape
    nc = shp[-1] // BLOCK_Q
    uc = u.reshape(shp[:-1] + (nc, BLOCK_Q))
    r = jnp.arange(BLOCK_Q)
    tri = (r[:, None] >= r[None, :]).astype(u.dtype)
    within = jnp.einsum('...cj,js->...cs', uc, tri, precision=lax.Precision.HIGHEST)
    c = jnp.arange(nc)
    later = (c[:, None] > c[None, :]).astype(u.dtype)
    suffix = jnp.einsum('...k,kc->...c', within[..., 0], later,
                        precision=lax.Precision.HIGHEST)
    return (within + suffix[..., None]).reshape(shp)

def _stick_breaking(cols):
    b, seq, _ = cols.shape
    q = _heads(cols[..., :MIX_WIDTH], SB_HEADS, SB_HEAD_DIM) * (SB_HEAD_DIM ** -0.5)
    k = _heads(cols[..., MIX_WIDTH:2 * MIX_WIDTH], SB_HEADS, SB_HEAD_DIM)
    v = _heads(cols[..., 2 * MIX_WIDTH:], SB_HEADS, SB_HEAD_DIM)
    outs = []
    for i in range(seq // BLOCK_Q):
        end = (i + 1) * BLOCK_Q
        qb = q[:, :, i * BLOCK_Q:end]
        z = jnp.einsum('bhqd,bhkd->bhqk', qb, k[:, :, :end]).astype(jnp.float32)
        qpos = i * BLOCK_Q + jnp.arange(BLOCK_Q)
        mask = jnp.arange(end)[None, :] < qpos[:, None]
        u = jnp.where(mask, jax.nn.softplus(z), 0.0)
        a = jnp.where(mask, jnp.exp(z - _rev_cumsum(u)), 0.0)
        outs.append(jnp.einsum('bhqk,bhkd->bhqd', a.astype(v.dtype), v[:, :, :end]))
    o = jnp.concatenate(outs, axis=2)
    return o.transpose(0, 2, 1, 3).reshape(b, seq, MIX_WIDTH)

def _diff_attention(cols, lam_q1, lam_k1, lam_q2, lam_k2, g_head, layer_idx):
    b, seq, _ = cols.shape
    scale = DIFF_HALF_DIM ** -0.5
    qh = cols[..., :MIX_WIDTH].reshape(b, seq, DIFF_HEADS, 2, DIFF_HALF_DIM) * scale
    kh = cols[..., MIX_WIDTH:2 * MIX_WIDTH].reshape(b, seq, DIFF_HEADS, 2, DIFF_HALF_DIM)
    q1 = qh[..., 0, :].transpose(0, 2, 1, 3)
    q2 = qh[..., 1, :].transpose(0, 2, 1, 3)
    k1 = kh[..., 0, :].transpose(0, 2, 1, 3)
    k2 = kh[..., 1, :].transpose(0, 2, 1, 3)
    v = _heads(cols[..., 2 * MIX_WIDTH:], DIFF_HEADS, 2 * DIFF_HALF_DIM)

    lambda_init = 0.8 - 0.6 * math.exp(-0.3 * layer_idx)
    f32 = jnp.float32
    lam = (jnp.exp(jnp.sum(lam_q1.astype(f32) * lam_k1.astype(f32)))
           - jnp.exp(jnp.sum(lam_q2.astype(f32) * lam_k2.astype(f32))) + lambda_init)
    slopes = 2.0 ** (-8.0 * jnp.arange(1, DIFF_HEADS + 1, dtype=f32) / DIFF_HEADS)

    outs = []
    for i in range(seq // BLOCK_Q):
        end = (i + 1) * BLOCK_Q
        qpos = i * BLOCK_Q + jnp.arange(BLOCK_Q)
        dist = (qpos[:, None] - jnp.arange(end)[None, :]).astype(f32)
        mask = dist >= 0.0
        bias = -slopes[:, None, None] * dist

        def probs(qq, kk):
            s = jnp.einsum('bhqd,bhkd->bhqk', qq[:, :, i * BLOCK_Q:end],
                           kk[:, :, :end]).astype(f32) + bias
            return jax.nn.softmax(jnp.where(mask, s, -jnp.inf), axis=-1)

        a = probs(q1, k1) - lam * probs(q2, k2)
        outs.append(jnp.einsum('bhqk,bhkd->bhqd', a.astype(v.dtype), v[:, :, :end]))
    o = jnp.concatenate(outs, axis=2).transpose(0, 2, 1, 3)
    o = _rmsnorm(o, g_head, HEAD_NORM_EPS) * (1.0 - lambda_init)
    return o.reshape(b, seq, MIX_WIDTH)

def _short_conv(cols, conv_w):
    gate_b = cols[..., :MIX_WIDTH]
    gate_c = cols[..., MIX_WIDTH:2 * MIX_WIDTH]
    h = cols[..., 2 * MIX_WIDTH:]
    u = gate_c * h
    y = lax.conv_general_dilated(
        u, conv_w[:, None, :].astype(u.dtype),
        window_strides=(1,), padding=[(CONV_WIDTH - 1, 0)],
        dimension_numbers=('NWC', 'WIO', 'NWC'),
        feature_group_count=MIX_WIDTH)
    return gate_b * y

def _memory_attention(mq, mem_n, w_kv):
    b, seq, _ = mq.shape
    kv = mem_n @ w_kv
    km = kv[..., :MEM_WIDTH].reshape(b, MEM_LEN, MEM_HEADS, MEM_HEAD_DIM)
    vm = kv[..., MEM_WIDTH:].reshape(b, MEM_LEN, MEM_HEADS, MEM_HEAD_DIM)
    q = mq.reshape(b, seq, MEM_HEADS, MEM_HEAD_DIM)
    s = jnp.einsum('bshd,bmhd->bhsm', q, km).astype(jnp.float32) * MEM_HEAD_DIM ** -0.5
    p = jax.nn.softmax(s, axis=-1)
    o = jnp.einsum('bhsm,bmhd->bshd', p.astype(vm.dtype), vm)
    return o.reshape(b, seq, MEM_WIDTH)

def _swiglu(x, w_in, w_out):
    gu = x @ w_in
    return (jax.nn.silu(gu[..., :D_FF_2]) * gu[..., D_FF_2:]) @ w_out

def second_inputs(seed: int = 0) -> dict:
    key = jax.random.key(seed)
    ks = jax.random.split(key, 17)
    f32 = jnp.float32
    n = lambda k, shape, s: jax.random.normal(k, shape, f32) * s
    return {
        "x": n(ks[0], (BATCH, SEQ, D_MODEL), 1.0),
        "mem": n(ks[1], (BATCH, MEM_LEN, D_MODEL), 1.0),
        "g_mix": 1.0 + n(ks[2], (DEPTH_2, D_MODEL), 0.02),
        "w_in": n(ks[3], (DEPTH_2, D_MODEL, IN_WIDTH), D_MODEL ** -0.5),
        "w_mem_kv": n(ks[4], (DEPTH_2, D_MODEL, 2 * MEM_WIDTH), D_MODEL ** -0.5),
        "w_o": n(ks[5], (DEPTH_2, OUT_IN_WIDTH, D_MODEL), OUT_IN_WIDTH ** -0.5),
        "g_ffn": 1.0 + n(ks[6], (DEPTH_2, D_MODEL), 0.02),
        "w_ffn_in": n(ks[7], (DEPTH_2, D_MODEL, 2 * D_FF_2), D_MODEL ** -0.5),
        "w_ffn_out": n(ks[8], (DEPTH_2, D_FF_2, D_MODEL), D_FF_2 ** -0.5),
        "lam_q1": n(ks[9], (N_DIFF, DIFF_HALF_DIM), LAMBDA_STD),
        "lam_k1": n(ks[10], (N_DIFF, DIFF_HALF_DIM), LAMBDA_STD),
        "lam_q2": n(ks[11], (N_DIFF, DIFF_HALF_DIM), LAMBDA_STD),
        "lam_k2": n(ks[12], (N_DIFF, DIFF_HALF_DIM), LAMBDA_STD),
        "g_diff_head": 1.0 + n(ks[13], (N_DIFF, 2 * DIFF_HALF_DIM), 0.02),
        "conv_w": n(ks[14], (N_CONV, CONV_WIDTH, D_MODEL), CONV_WIDTH ** -0.5),
        "g_mem": 1.0 + n(ks[15], (D_MODEL,), 0.02),
        "g_final": 1.0 + n(ks[16], (D_MODEL,), 0.02),
    }

def second_block(x, mem, g_mix, w_in, w_mem_kv, w_o, g_ffn, w_ffn_in, w_ffn_out,
              lam_q1, lam_k1, lam_q2, lam_k2, g_diff_head, conv_w, g_mem, g_final):
    mem_n = _rmsnorm(mem, g_mem)
    for i in range(DEPTH_2):
        kind = i % N_MIXERS
        j = i // N_MIXERS
        hn = _rmsnorm(x, g_mix[i])
        proj = hn @ w_in[i]
        cols, mq = proj[..., :3 * MIX_WIDTH], proj[..., 3 * MIX_WIDTH:]
        if kind == 0:
            mix = _stick_breaking(cols)
        elif kind == 1:
            mix = _diff_attention(cols, lam_q1[j], lam_k1[j], lam_q2[j], lam_k2[j],
                                  g_diff_head[j], i)
        else:
            mix = _short_conv(cols, conv_w[j])
        mo = _memory_attention(mq, mem_n, w_mem_kv[i])
        x = x + jnp.concatenate([mix, mo], axis=-1) @ w_o[i]
        x = x + _swiglu(_rmsnorm(x, g_ffn[i]), w_ffn_in[i], w_ffn_out[i])
    return _rmsnorm(x, g_final)


def setup_inputs(seed=0):
    out = dict(first_inputs(seed))
    for name, value in second_inputs(seed + 1).items():
        if name != "x":
            out[name + "_2"] = value
    return out


def reference(
    x, norm_mix_g, w_in, ssm_lam_re, ssm_lam_im, ssm_log_dt, ssm_b_re, ssm_b_im, ssm_c_re,
    ssm_c_im, ssm_d, ssm_w_glu, ssm_b_glu, attn_rel_bias, norm_ssm_out_g, norm_att_out_g, w_out,
    norm_ffn_g, w_gate, w_up, w_down, norm_final_g, mem_2, g_mix_2, w_in_2, w_mem_kv_2, w_o_2,
    g_ffn_2, w_ffn_in_2, w_ffn_out_2, lam_q1_2, lam_k1_2, lam_q2_2, lam_k2_2, g_diff_head_2,
    conv_w_2, g_mem_2, g_final_2,
):
    x = first_block(
        x, norm_mix_g, w_in, ssm_lam_re, ssm_lam_im, ssm_log_dt, ssm_b_re, ssm_b_im, ssm_c_re,
        ssm_c_im, ssm_d, ssm_w_glu, ssm_b_glu, attn_rel_bias, norm_ssm_out_g, norm_att_out_g,
        w_out, norm_ffn_g, w_gate, w_up, w_down, norm_final_g,
    )
    return second_block(
        x, mem_2, g_mix_2, w_in_2, w_mem_kv_2, w_o_2, g_ffn_2, w_ffn_in_2, w_ffn_out_2,
        lam_q1_2, lam_k1_2, lam_q2_2, lam_k2_2, g_diff_head_2, conv_w_2, g_mem_2, g_final_2,
    )


_drawn_inputs = setup_inputs


def setup_inputs(seed=0):
    import zlib

    import numpy as np

    out = dict(_drawn_inputs(seed))
    spreads = {}
    factors = {'ssm_lam_re': 8.0,
     'ssm_b_glu': 6.737,
     'lam_k1_2': 8.0,
     'g_diff_head_2': 4.678,
     'g_mem_2': 8.0,
     'g_final_2': 2.741}
    for name, (base, spread) in spreads.items():
        noise = np.random.default_rng([zlib.crc32(name.encode()), seed]).standard_normal(out[name].shape)
        drawn = base * np.exp(spread * noise) if base else spread * noise
        out[name] = __import__('jax').numpy.asarray(drawn.astype(out[name].dtype))
    for name, factor in factors.items():
        out[name] = (out[name] * factor).astype(out[name].dtype)
    return out
```

```python
import math
from contextlib import ExitStack

import concourse.bass as bass
from concourse import mybir

F32 = mybir.dt.float32
F32R = mybir.dt.float32r
ALU = mybir.AluOpType
ACT = mybir.ActivationFunctionType
AX = mybir.AxisListType

P = 128
T = 512
TT = T // P
D = 1024
KD = D // P
FF = 2816
KF = FF // P
DS = 512
GRP, HG, NS = 32, 16, 64
ST = GRP * NS // P
NH1, DH1 = 8, 64
MAXREL = 128
NL = 4
NH2, DH2 = 8, 128
MEM, MH, MD = 256, 4, 64
WIN2 = 3 * D + MH * MD
KO = (D + MH * MD) // P
BANK = 512
UNIT = 2048
NEG, BIG = -1e30, 3e38
EPS, HEPS = 1e-6, 1e-5

U_IN1, U_GLU, U_OUT1 = 0, 8, 9
U_GU1 = U_OUT1 + 4
U_DN1 = U_GU1 + 2 * (FF // 256)
U_KV = U_DN1 + 12
U_L0 = U_KV + 2 * NL
L_QK, L_V, L_MQ, L_O, L_GU, L_DN = 0, 8, 12, 13, 21, 43
PER_LAYER = 55
UNITS = U_L0 + NL * PER_LAYER

ZK = {0: 0, 1: 512, 3: 896, 2: 1024}
ZQ = {0: 0, 2: 128, 3: 512, 1: 1024}
ZW = 1280


def wk(j):
    return T - P * j


def wq(i):
    return P * (i + 1)


C_MIX1, C_FFN1, C_FIN1, C_MIX2, C_FFN2, C_MEM, C_FIN2 = 0, 8, 16, 24, 56, 88, 96
C_SSM, C_ATT, C_BGLU, C_D, C_DIFF, C_LAM, C_END = 104, 108, 112, 116, 120, 122, 126
C_CONV = 126


def has_h(r):
    return r not in (2, 11)


def h_index(r):
    return sum(has_h(q) for q in range(r))


def gain_col(r):
    if r == 0:
        return C_MIX1
    if r == 1:
        return C_FFN1
    if r % 2:
        return C_MIX2 + KD * ((r - 3) // 2)
    return C_FFN2 + KD * ((r - 4) // 2)


def loop(eng, n, body, peel=1):
    for i in range(peel):
        body(i)
    if n > peel:
        with eng.Fori(peel, n) as i:
            body(i)


def build(nc, A, out, ext_dram):
    with ExitStack() as ctx:
        sems = {}

        def S(name):
            if name not in sems:
                sems[name] = ctx.enter_context(nc.semaphore(name))
            return sems[name]

        top = [1152]

        def at(name, offset, shape, dt=F32):
            return nc.alloc_sbuf_tensor_at(name, shape, dt, offset=offset)

        def place(nbytes):
            o = top[0]
            top[0] += (nbytes + 31) // 32 * 32
            return o

        x = at("x", place(KD * T * 4), [P, KD, T])
        H0 = place(2 * KD * T * 4)
        hh = at("hh", H0, [P, KD, T], F32R)
        hl = at("hl", H0 + KD * T * 4, [P, KD, T], F32R)
        A0 = place(KF * 2 * T * 4)
        act2 = at("act2", A0, [P, KF, 2, T], F32R)
        raw = at("raw", place(2 * UNIT * 4), [P, 2, UNIT])
        whi = at("whi", place(2 * UNIT * 4), [P, 2, UNIT], F32R)
        wlo = at("wlo", place(2 * UNIT * 4), [P, 2, UNIT], F32R)
        KV0 = place(2 * NL * 2 * MEM * 4)
        km = at("km", KV0, [P, NL, 2, MEM])
        vm = at("vm", KV0 + NL * 2 * MEM * 4, [P, NL, 2, MEM])
        GS0 = place(2 * T * 4)
        gs = at("gs", GS0, [P, 2, T])
        mq = at("mq", GS0, [P, 2, T])
        US0 = place(2 * T * 4)
        us = at("us", US0, [P, 2, T])
        rstd = at("rstd", place(T * 4), [P, T])
        sqacc = at("sqacc", place(T * 4), [P, T])
        sqb = at("sqb", place(2 * T * 4), [P, 2, T])
        ident = at("ident", place(P * 4), [P, P])
        ones = at("ones", place(P * 4), [P, P])
        negtri = at("negtri", place(P * 4), [P, P], F32R)
        negones = at("negones", place(P * 4), [P, P], F32R)
        mask = at("mask", place(P * 4), [P, P])
        cap = at("cap", place(P * 4), [P, P])
        cols = at("cols", place(152 * 4), [P, 152])
        rstdc = at("rstdc", place(TT * 4), [P, TT])
        sd = at("sd", place(TT * 4), [P, TT])
        epsc = at("epsc", place(4), [P, 1])
        hepsc = at("hepsc", place(4), [P, 1])
        mx = at("mx", place(32), [P, 2, 4])
        ngm = at("ngm", place(2 * 16), [P, 2, 4])
        sums = at("sums", place(2 * 16), [P, 2, 4])
        rec = at("rec", place(2 * 16), [P, 2, 4])
        lam = at("lam", place(32), [P, 8])
        gdiff = at("gdiff", place(8), [P, 2])
        ssp = at("ssp", place(3 * 64), [P, 3, 16])
        rmod = at("rmod", place(64), [P, ST])
        cst = at("cst", place(P * 4), [P, P])
        flip = at("flip", place(P * 4), [P, P])
        assert top[0] <= 229344, top[0]

        er = at("er", A0, [P, ST, T])
        ei = at("ei", A0 + ST * T * 4, [P, ST, T])
        QKV1 = A0 + 65536
        q1 = at("q1", QKV1, [P, 4, T])
        k1 = at("k1", QKV1 + 8192, [P, 4, T])
        v1 = at("v1", QKV1 + 16384, [P, TT, T])
        xtok = at("xtok", QKV1, [P, TT, D])
        yu = at("yu", KV0, [P, 4, T])
        ya = at("ya", KV0 + 8192, [P, 4, T])
        QKV2 = A0 + 10 * 2 * T * 4
        q2 = at("q2", QKV2, [P, 8, T])
        k2 = at("k2", QKV2 + 16384, [P, 8, T])
        v2 = at("v2", QKV2 + 32768, [P, TT, D])
        vf = at("vf", QKV2 + 32768, [P, 8, T])
        mtok = at("mtok", KV0, [P, 2, D])
        mh = at("mh", A0, [P, KD, MEM], F32R)
        ml = at("ml", A0 + 8192, [P, KD, MEM], F32R)
        otok = at("otok", A0, [P, TT, D])

        ps = ctx.enter_context(nc.psum_tensor("ps", [P, 8 * BANK], F32))

        def bank(b, w=BANK, off=0):
            return ps[:, b * BANK + off:b * BANK + off + w]

        def col(c, n=1):
            return cols[:, c:c + n]

        w_in1 = A["w_in"][0].rearrange("(k p) n -> p k n", p=P)
        w_glu = A["ssm_w_glu"][0].rearrange("(k p) n -> p k n", p=P)
        w_out1 = A["w_out"][0].rearrange("(k p) n -> p k n", p=P)
        w_g1 = A["w_gate"][0].rearrange("(k p) n -> p k n", p=P)
        w_u1 = A["w_up"][0].rearrange("(k p) n -> p k n", p=P)
        w_d1 = A["w_down"][0].rearrange("(k p) n -> p k n", p=P)
        w_in2 = [A["w_in_2"][l].rearrange("(k p) n -> p k n", p=P) for l in range(NL)]
        w_kv2 = [A["w_mem_kv_2"][l].rearrange("(k p) n -> p k n", p=P) for l in range(NL)]
        w_o2 = [A["w_o_2"][l].rearrange("(k p) n -> p k n", p=P) for l in range(NL)]
        w_f2 = [A["w_ffn_in_2"][l].rearrange("(k p) n -> p k n", p=P) for l in range(NL)]
        w_d2 = [A["w_ffn_out_2"][l].rearrange("(k p) n -> p k n", p=P) for l in range(NL)]

        loaded = [S("loaded0"), S("loaded1")]
        hi_made, lo_made, unit_used = S("hi_made"), S("lo_made"), S("unit_used")
        acc_free = S("acc_free")
        resid_done, x_new, h_hi, h_ready = S("resid_done"), S("x_new"), S("h_hi"), S("h_ready")
        sq_ready, sq_summed = S("sq_ready"), S("sq_summed")
        ssum_done, sd_ready, rstd_ready = S("ssum_done"), S("sd_ready"), S("rstd_ready")
        silu_done, act_step, act_ready = S("silu_done"), S("act_step"), S("act_ready")
        mix_hi, mix_ready = S("mix_hi"), S("mix_ready")
        const_step, const_ready = S("const_step"), S("const_ready")


        G_GU1, G_KV, G_L0 = 8, 30, 38

        def g_in(l):
            return G_L0 + 35 * l

        def g_gu(l):
            return g_in(l) + 13

        def u_layer(l):
            return U_L0 + PER_LAYER * l

        braw = at("braw", QKV1 + 16384, [P, 2, ST, HG])
        bpre = at("bpre", QKV1 + 16384 + 2048, [P, 2, ST, 32])
        prep = at("prep", place(20 * ST * 4), [P, 20, ST])
        rows_a = at("rows_a", KV0 + 8192, [P, P])
        rows_b = at("rows_b", KV0 + 8192 + 512, [P, P])
        rows_s = at("rows_s", KV0 + 8192 + 1024, [P, 3, P])
        craw = at("craw", KV0 + 8192 + 2560, [P, 2, 4, 2, NS])
        ext = at("ext", H0 + 32768 - 2560, [P, 640])
        ldt = at("ldt", KV0 + 8192 + 6656, [P, 2])
        bt = at("bt", GS0, [P, 4, 2, P])
        ct = at("ct", US0, [P, ST, 2, 32])
        pbuf = [at(f"pbuf{i}", H0 + 5120 * i, [P, ZW]) for i in range(2)]
        ptb = [at(f"ptb{i}", H0 + 10240 + 5120 * i, [P, ZW]) for i in range(2)]
        hank = [at(f"hank{i}", H0 + 20480 + 2048 * i, [P, T]) for i in range(2)]
        bsb = [at(f"bsb{i}", H0 + 24576 + 2048 * i, [P, T]) for i in range(2)]
        sm = [at(f"sm{i}", H0 + 2048 * i, [P, T]) for i in range(4)]
        sx = [at(f"sx{i}", H0 + 8192 + 2048 * i, [P, T]) for i in range(2)]
        ss = [at(f"ss{i}", H0 + 12288 + 2048 * i, [P, T]) for i in range(2)]
        sn = [at(f"sn{i}", H0 + 16384 + 2048 * i, [P, T]) for i in range(4)]
        sy = [at(f"sy{i}", H0 + 24576 + 2048 * i, [P, T]) for i in range(2)]
        gh = at("gh", H0, [P, 4, T], F32R)
        gl = at("gl", H0 + 8192, [P, 4, T], F32R)
        sig = at("sig", H0 + 16384, [P, 4, T])
        ze = at("ze", H0, [P, ZW])
        zu = at("zu", H0 + 5120, [P, ZW])
        uh = [at(f"uh{i}", H0 + 10240 + 10240 * i, [P, ZW], F32R) for i in range(2)]
        ul = [at(f"ul{i}", H0 + 15360 + 10240 * i, [P, ZW], F32R) for i in range(2)]
        az = [at(f"az{i}", H0 + 10240 + 10240 * i, [P, ZW]) for i in range(2)]
        osq = [at(f"osq{i}", H0 + 20480 + 2048 * i, [P, T]) for i in range(2)]
        dbias = at("dbias", H0 + 24576, [P, T])
        dist = at("dist", H0 + 26624, [P, T])
        dneg = at("dneg", H0 + 28672, [P, T])
        ors = at("ors", H0 + 30720, [P, T])
        mp = [at(f"mp{i}", H0 + 4096 * i, [P, 4, MEM]) for i in range(2)]
        mt = [at(f"mt{i}", H0 + 8192 + 4096 * i, [P, 2, T]) for i in range(2)]
        cv = at("cv", H0, [P, T + 2])
        cy = [at(f"cy{i}", H0 + 4096 + 2048 * i, [P, T]) for i in range(2)]

        def bc(ap2, n):
            m = ap2.shape[1]
            return ap2.rearrange("p (a m) -> p a m", a=1).broadcast_to([P, n, m])

        def bcl(ap2, n):
            m = ap2.shape[1]
            return ap2.rearrange("p (m a) -> p m a", a=1).broadcast_to([P, m, n])

        n_small = [0]
        LAMBDA_INIT = 0.8 - 0.6 * math.exp(-0.3)
        block = ctx.enter_context(nc.Block())

        @block.sync
        def _(sp):
            sp.dma_start(xtok[:, :, :], A["x"][0].rearrange("(t p) d -> p t d", p=P)).then_inc(S("x_loaded"), 16)

            def load(slot, kn, cn, src, need):
                dst = raw[:, slot, 0:kn * cn].rearrange("p (k n) -> p k n", n=cn)
                if need is not None:
                    sp.wait_ge(lo_made, need)
                sp.dma_start(dst, src).then_inc(loaded[slot], 16)

            def pair_loop(n, u0, kn, cn, src_of, peel=0, per=2):
                def turn(i):
                    where, need = [], []
                    for j in range(per):
                        w, k0, kk, c0, step = src_of(j)
                        where.append((w, k0, kk, c0 + step * i if isinstance(i, int) else sp.snap(i * step + c0)))
                        u = u0 + j
                        if isinstance(i, int):
                            v = u + per * i - 1
                            need.append(v if v > 0 else None)
                        else:
                            need.append(sp.snap(i * per + (u - 1)))
                    for j in range(per):
                        w, k0, kk, off = where[j]
                        load((u0 + j) % 2, kk, cn, w[:, k0:k0 + kk, bass.ds(off, cn)], need[j])
                loop(sp, n, turn, peel)

            def swiglu(u0, wg, g0, wu, u1, wd, between=None):
                pair_loop(FF // 256, u0, KD, 256, lambda j: ((wg, 0, KD, g0, 256), (wu, 0, KD, u1, 256))[j])
                if between:
                    between()
                pair_loop(2, u0 + 22, 4, 512, lambda j: (wd, 4 * j, min(4, KF - 4 * j), 0, 512), per=6)

            pair_loop(4, U_IN1, KD, 256, lambda j: (w_in1, 0, KD, 256 * j, 512), peel=2)
            load(U_GLU % 2, 4, 512, w_glu[:, 0:4, :], U_GLU - 1)
            pair_loop(2, U_OUT1, KD, 256, lambda j: (w_out1, 0, KD, 256 * j, 512))

            def memory():
                sp.wait_ge(S("mix_ready"), 8)
                sp.dma_start(mtok[:, :, :], A["mem_2"][0].rearrange("(t p) d -> p t d", p=P)).then_inc(S("mem_loaded"), 16)
            swiglu(U_GU1, w_g1, 0, w_u1, 0, w_d1, memory)
            for l in range(NL):
                for j in range(2):
                    u = U_KV + 2 * l + j
                    load(u % 2, KD, 256, w_kv2[l][:, :, 256 * j:256 * j + 256], u - 1)
            for l in range(NL):
                u0 = u_layer(l)
                pair_loop(6, u0, KD, 256, lambda j: (w_in2[l], 0, KD, 256 * j, 512))
                load((u0 + L_MQ) % 2, KD, 256, w_in2[l][:, :, 3 * D:3 * D + 256], u0 + L_MQ - 1)
                pair_loop(4, u0 + L_O, 5, 256, lambda j: (w_o2[l], 5 * j, 5, 0, 256))
                swiglu(u0 + L_GU, w_f2[l], 0, w_f2[l], FF, w_d2[l])
            for t in range(TT):
                sp.wait_ge(S("out_tile"), 2 * (t + 1))
                sp.dma_start(out[P * t:P * t + P, :], otok[:, t, :]).then_inc(S("stored"), 16)
            sp.wait_ge(S("stored"), 16 * TT)

        @block.gpsimd
        def _(pool):
            g = nc.gpsimd
            g.memset(ident[:, :], 0.0).then_inc(const_step, 1)
            g.memset(ones[:, :], 1.0).then_inc(const_step, 1)
            g.memset(flip[:, :], 0.0).then_inc(const_step, 1)
            g.memset(mask[:, :], 1.0).then_inc(const_step, 1)
            g.memset(cap[:, :], BIG).then_inc(const_step, 1)
            g.memset(cst[:, :], -1.0).then_inc(const_step, 1)
            g.memset(epsc[:, :], EPS).then_inc(const_step, 1)
            g.memset(hepsc[:, :], HEPS).then_inc(const_step, 1)
            g.memset(bpre[:, :, :, :], 0.0).then_inc(const_step, 1)
            g.memset(ct[:, :, :, :], 0.0).then_inc(const_step, 1)
            pool.wait_ge(const_step, 10)
            g.affine_select(out=ident[:, :], in_=ident[:, :], compare_op=ALU.not_equal, fill=1.0,
                            base=0, pattern=[[-1, P]], channel_multiplier=1).then_inc(const_ready, 1)
            g.affine_select(out=flip[:, :], in_=flip[:, :], compare_op=ALU.not_equal, fill=1.0,
                            base=-(P - 1), pattern=[[1, P]], channel_multiplier=1).then_inc(const_ready, 1)
            g.affine_select(out=mask[:, :], in_=mask[:, :], compare_op=ALU.is_gt, fill=0.0,
                            base=0, pattern=[[1, P]], channel_multiplier=-1).then_inc(const_ready, 1)
            g.affine_select(out=cap[:, :], in_=cap[:, :], compare_op=ALU.is_gt, fill=NEG,
                            base=0, pattern=[[1, P]], channel_multiplier=-1).then_inc(const_ready, 1)
            g.affine_select(out=cst[:, :], in_=cst[:, :], compare_op=ALU.is_ge, fill=0.0,
                            base=0, pattern=[[-1, P]], channel_multiplier=1).then_inc(const_ready, 1)

            def low(slot, need):
                pool.wait_ge(hi_made, need)
                g.tensor_tensor(wlo[:, slot, :], raw[:, slot, :], whi[:, slot, :].bitcast(F32),
                                ALU.subtract).then_inc(lo_made, 1)

            loop(pool, 5, lambda i: [low(j, 2 * i + j + 1) for j in range(2)], peel=1)
            for t in range(ST + 1):
                if t < ST:
                    pool.wait_ge(S("ssm_m"), 4 * (t + 1))
                    if t:
                        pool.wait_ge(S("ssm_scan"), 2 * t)
                    g.tensor_tensor(sx[0][:, :], sm[0][:, :], sm[1][:, :], ALU.add).then_inc(S("ssm_x"), 1)
                    g.tensor_tensor(sx[1][:, :], sm[2][:, :], sm[3][:, :], ALU.subtract).then_inc(S("ssm_x"), 1)
                if t:
                    pool.wait_ge(S("ssm_n"), 4 * t)
                    if t > 1:
                        pool.wait_ge(S("ssm_yd"), t - 1)
                    g.tensor_tensor(sy[0][:, :], sn[0][:, :], sn[1][:, :], ALU.subtract).then_inc(S("ssm_y"), 1)
                    g.tensor_tensor(sy[1][:, :], sn[2][:, :], sn[3][:, :], ALU.add).then_inc(S("ssm_y"), 1)
            with pool.Fori(5, UNITS // 2) as i:
                for j in range(2):
                    low(j, i * 2 + (j + 1))
            low(0, UNITS)

        @block.scalar
        def _(act):
            a = nc.scalar

            def small(dst, src):
                n_small[0] += 1
                act.dma_start(dst, src).then_inc(S("small_loaded"), 16)

            for k, name in ((0, "ssm_lam_re"), (1, "ssm_lam_im")):
                act.dma_start(rows_s[0:ST, k, :], A[name][0].rearrange("(i g) s -> i (g s)", g=2)).then_inc(S("ssm_loaded"), 16)
            act.dma_start(ldt[0:ST, :], A["ssm_log_dt"][0].rearrange("(i g) -> i g", g=2)).then_inc(S("ssm_loaded"), 16)

            def vec(c, name, n, w=None):
                v = A[name] if w is None else w
                small(rows_a[c:c + n, :], v)
            for c, name, n in ((C_MIX1, "norm_mix_g", 8), (C_FFN1, "norm_ffn_g", 8),
                               (C_SSM, "norm_ssm_out_g", 4), (C_ATT, "norm_att_out_g", 4),
                               (C_BGLU, "ssm_b_glu", 4), (C_DIFF, "g_diff_head_2", 2)):
                vec(c, name, n, A[name][0].rearrange("(t p) -> t p", p=P))
            for c, name in ((C_FIN1, "norm_final_g"), (C_MEM, "g_mem_2"), (C_FIN2, "g_final_2")):
                vec(c, name, 8, A[name].rearrange("(t p) -> t p", p=P))
            for c, name in ((C_MIX2, "g_mix_2"), (C_FFN2, "g_ffn_2")):
                vec(c, name, 32, A[name].rearrange("l (t p) -> (l t) p", p=P))
            vec(C_D, "ssm_d", 4, A["ssm_d"][0].rearrange("(t g) h -> t (g h)", t=4))
            for i, name in enumerate(("lam_q1_2", "lam_k1_2", "lam_q2_2", "lam_k2_2")):
                vec(C_LAM + i, name, 1, A[name])
            small(rows_b[0:24, :], A["conv_w_2"][0].rearrange("i (t p) -> (i t) p", p=P))
            for r, name in enumerate(("ssm_b_re", "ssm_b_im")):
                small(braw[:, r, :, :], A[name][0].rearrange("(i g) s h -> (g s) i h", g=2))
            for r, name in enumerate(("ssm_c_re", "ssm_c_im")):
                for d in range(2):
                    small(craw[:, r, :, d, :], A[name][0].rearrange("(c g) h s -> (g h) c s", c=4))
            small(ext[0:NH1, 383:639], A["attn_rel_bias"][0][:, 0:256])

            def high(slot, load_need, used_need):
                act.wait_ge(loaded[slot], load_need)
                if used_need is not None:
                    act.wait_ge(unit_used, used_need)
                a.activation(whi[:, slot, :], raw[:, slot, :], ACT.Copy).then_inc(hi_made, 1)

            def ahead(u0, i=0, per=0, j=0):
                v = u0 + j + 2
                if isinstance(i, int):
                    v += per * i
                    if v < UNITS:
                        high(v % 2, 16 * (v // 2 + 1), v - 1)
                else:
                    high(v % 2, i * (8 * per) + 16 * (v // 2 + 1), i * per + (v - 1))

            def residual(r, tiles=range(KD)):
                for t in tiles:
                    n = KD * r + t
                    act.wait_ge(x_new, n + 1)
                    if has_h(r):
                        a.activation(hh[:, t, :], x[:, t, :], ACT.Identity,
                                     scale=col(gain_col(r) + t)).then_inc(h_hi, 1)
                    if n >= 2:
                        act.wait_ge(sq_summed, n - 1)
                    a.activation(sqb[:, n % 2, :], x[:, t, :], ACT.Square).then_inc(sq_ready, 1)

            def norm(r, b=6):
                act.wait_ge(ssum_done, r + 1)
                a.activation(sd[:, :], bank(b + 1, TT), ACT.Sqrt, bias=epsc[:, :], scale=1.0 / D).then_inc(sd_ready, 1)

            def swiglu(s, u0, gc, r, between=None):
                def turn(i):
                    first = isinstance(i, int) and i == 0
                    if first:
                        norm(r, 0)
                        ahead(u0)
                    act.wait_ge(acc_free, gc + 1 + i * 2 if isinstance(i, int) else i * 2 + (gc + 1))
                    a.activation(gs[:, :, :], gs[:, :, :], ACT.Silu).then_inc(silu_done, 1)
                    for j in range(1 if first else 0, 2):
                        ahead(u0, i, 2, j)
                loop(act, FF // 256, turn)
                for i in range(2):
                    for j in range(6):
                        if 6 * i + j == 11:
                            residual(r + 1, range(4, 7))
                        ahead(u0 + 22, i, 6, j)
                    if i == 0:
                        if between:
                            between()
                        residual(r + 1, range(4))
                residual(r + 1, range(7, 8))

            high(0, 16, None)
            high(1, 16, None)

            act.wait_ge(S("ssp_ready"), 1)
            a.activation(ssp[:, 2, :], ssp[:, 2, :], ACT.Exp).then_inc(S("dt_ready"), 1)
            act.wait_ge(S("a_ready"), 1)
            a.activation(rmod[:, :], prep[:, 0, :], ACT.Exp).then_inc(S("rmod_ready"), 1)
            act.wait_ge(S("rows_ready"), 1)
            act.dma_start(ext_dram[:, 0:639], ext[0:NH1, 0:639]).then_inc(S("ext_stored"), 16)
            residual(0)
            norm(0)
            for u in range(8):
                ahead(u)

            def hankel(h):
                src = bass.AP(tensor=ext_dram.tensor, offset=640 * h, ap=[[1, P], [1, T]])
                act.dma_start(hank[h % 2][:, :], src).then_inc(S(f"hankel{h % 2}"), 16)

            act.wait_ge(S("ext_stored"), 16)
            act.wait_ge(unit_used, 8)
            hankel(0)
            hankel(1)

            def relcopy(h):
                act.wait_ge(S("a1_bias"), h + 1)
                if h >= 2:
                    act.wait_ge(S("a1_s"), 4 * (h - 1))
                b = bsb[h % 2]
                a.activation(b[:, 0:448], bank(7, 448), ACT.Copy).then_inc(S("a1_bcopy"), 1)
                a.activation(b[64:128, 448:512], ps[64:128, 7 * BANK + 448:8 * BANK], ACT.Copy).then_inc(S("a1_bcopy"), 1)

            for t in range(NH1 + 1):
                if t < NH1:
                    relcopy(t)
                    if t + 2 < NH1:
                        hankel(t + 2)
                    act.wait_ge(S("a1_ngm"), t + 1)
                    for i in range(4):
                        z = pbuf[t % 2][:, ZQ[i]:ZQ[i] + wq(i)]
                        a.activation(z, z, ACT.Exp, bias=ngm[:, t % 2, i:i + 1],
                                     accum_out=sums[:, t % 2, i:i + 1]).then_inc(S("a1_exp"), 1)
                if t:
                    act.wait_ge(S("a1_tr"), t)
                    if t >= 3:
                        act.wait_ge(S("a1_pv"), t - 2)
                    a.activation(ptb[(t - 1) % 2][:, :], ps[:, 3 * BANK:3 * BANK + ZW], ACT.Copy).then_inc(S("a1_pt"), 1)

            for c in range(4):
                act.wait_ge(S("ssm_skip"), c + 1)
                a.activation(yu[:, c, :], yu[:, c, :], ACT.Gelu_apprx_tanh).then_inc(S("gelu"), 1)
                act.wait_ge(S("gelu"), c + 1)
                a.activation(gh[:, c, :], yu[:, c, :], ACT.Copy).then_inc(S("gelu_hi"), 1)
            ahead(U_GLU)
            for c in range(4):
                if c < 3:
                    act.wait_ge(S("glu_done"), c + 1)
                else:
                    act.wait_ge(unit_used, U_GLU + 1)
                a.activation(sig[:, c, :], bank(c), ACT.Sigmoid, bias=col(C_BGLU + c)).then_inc(S("sig"), 1)

            def half_norm(n, src):
                for c in range(4):
                    m = 4 * n + c
                    if n == 0:
                        act.wait_ge(S("ya_ready"), c + 1)
                    else:
                        act.wait_ge(S("y_gated"), c + 1)
                    if m >= 2:
                        act.wait_ge(S("hn_sum"), m - 1)
                    a.activation(sqb[:, m % 2, :], src[:, c, :], ACT.Square).then_inc(S("hn_sq"), 1)
                act.wait_ge(S("hn_ssum"), n + 1)
                a.activation(rstd[:, :], bank(6), ACT.Sqrt, bias=epsc[:, :], scale=1.0 / DS).then_inc(S("hn_sd"), 1)
                for c in range(4):
                    m = 4 * n + c
                    act.wait_ge(S("hn_y"), m + 1)
                    slot = (4 if n == 0 else 0) + c
                    a.activation(act2[:, slot, 0, :], src[:, c, :], ACT.Copy).then_inc(mix_hi, 1)
            half_norm(0, ya)
            half_norm(1, yu)

            for j in range(4):
                ahead(U_OUT1 + j)
                residual(1, (2 * j, 2 * j + 1))

            def memory_norm():
                act.wait_ge(S("mem_loaded"), 16)
                for t in range(2):
                    a.activation(gs[:, :, :].rearrange("p a n -> p (a n)"), mtok[:, t, :], ACT.Square,
                                 accum_out=sums[:, 0, t:t + 1]).then_inc(S("mem_sq"), 1)
                    act.wait_ge(S("mem_sq"), t + 1)
                a.activation(rec[:, 0, 0:2], sums[:, 0, 0:2], ACT.Sqrt, bias=epsc[:, :], scale=1.0 / D).then_inc(S("mem_sd"), 1)
            swiglu(0, U_GU1, G_GU1, 1, memory_norm)
            for k in range(KD):
                act.wait_ge(S("mem_tr"), k + 1)
                a.activation(mh[:, k, :], bank(k, MEM), ACT.Identity, scale=col(C_MEM + k)).then_inc(S("mem_hi"), 1)
            norm(2)
            residual(3)
            for u in range(8):
                ahead(U_KV + u)

            def memory_attention(l):
                for h in range(MH + 1):
                    n = MH * l + h
                    if h < MH:
                        act.wait_ge(S("m_ngm"), n + 1)
                        for i in range(4):
                            a.activation(mp[h % 2][:, i, :], ps[:, MEM * i + 1024 * (h % 2):MEM * (i + 1) + 1024 * (h % 2)],
                                         ACT.Exp, bias=ngm[:, h % 2, i:i + 1], scale=MD ** -0.5,
                                         accum_out=sums[:, h % 2, i:i + 1]).then_inc(S("m_exp"), 1)
                    if h:
                        act.wait_ge(S("m_tr"), n)
                        a.activation(mt[(h - 1) % 2][:, :, :], ps[:, 4 * BANK:6 * BANK].rearrange("p (a n) -> p a n", a=2), ACT.Copy).then_inc(S("m_pt"), 1)
                for f in range(2):
                    act.wait_ge(S("m_pv"), MH * l + 2 * f + 2)
                    a.activation(act2[:, 8 + f, 0, :], bank(6 + f), ACT.Copy).then_inc(mix_hi, 1)

            def stick(idx):
                for t in range(NH2 + 2):
                    n = NH2 * idx + t
                    z = ps[:, 3 * BANK * (t % 2):3 * BANK * (t % 2) + ZW]
                    if t < NH2:
                        act.wait_ge(S("k_z"), n + 1)
                        if t:
                            act.wait_ge(S("k_u"), 3 * n)
                        a.activation(ze[:, :], z, ACT.Abs).then_inc(S("k_e"), 1)
                        act.wait_ge(S("k_e"), 3 * n + 1)
                        a.activation(ze[:, :], ze[:, :], ACT.Exp, scale=-1.0).then_inc(S("k_e"), 1)
                        act.wait_ge(S("k_e"), 3 * n + 2)
                        a.activation(ze[:, :], ze[:, :], ACT.Ln, bias=1.0).then_inc(S("k_e"), 1)
                    if 1 <= t <= NH2:
                        act.wait_ge(S("k_cap"), 2 * n)
                        a.activation(az[(t - 1) % 2][:, :], ps[:, 3 * BANK * ((t - 1) % 2):3 * BANK * ((t - 1) % 2) + ZW], ACT.Exp).then_inc(S("k_a"), 1)
                    if t < NH2:
                        act.wait_ge(S("k_u"), 3 * (n + 1))
                        if t >= 2:
                            act.wait_ge(S("k_o"), n - 1)
                        a.activation(uh[t % 2][:, :], zu[:, :], ACT.Copy).then_inc(S("k_uh"), 1)
                    if t >= 2:
                        act.wait_ge(S("k_o"), n - 1)
                        a.activation(act2[:, t - 2, 0, :], bank(6 + t % 2), ACT.Copy).then_inc(mix_hi, 1)

            def differential():
                act.wait_ge(S("d_lamsum"), 1)
                a.activation(lam[:, 2:4], bank(3, 2), ACT.Exp).then_inc(S("d_lamexp"), 1)
                for hd in range(4):
                    for c in range(2):
                        m = 2 * hd + c
                        act.wait_ge(S("d_ngm"), m + 1)
                        for i in range(4):
                            z = pbuf[c][:, ZQ[i]:ZQ[i] + wq(i)]
                            a.activation(z, z, ACT.Exp, bias=ngm[:, c, i:i + 1],
                                         accum_out=sums[:, c, i:i + 1]).then_inc(S("d_exp"), 1)
                    act.wait_ge(S("d_tr"), hd + 1)
                    a.activation(ptb[0][:, :], ps[:, 3 * BANK:3 * BANK + ZW], ACT.Copy).then_inc(S("d_pt"), 1)
                    act.wait_ge(S("d_pv"), hd + 1)
                    for d in range(2):
                        a.activation(osq[d][:, :], bank(6 + d), ACT.Square).then_inc(S("d_sq"), 1)
                    act.wait_ge(S("d_ssum"), hd + 1)
                    a.activation(ors[:, :], bank(3), ACT.Sqrt, bias=hepsc[:, :], scale=1.0 / 256).then_inc(S("d_sd"), 1)
                    for d in range(2):
                        act.wait_ge(S("d_on"), 2 * hd + d + 1)
                        a.activation(act2[:, 2 * hd + d, 0, :], us[:, d, :], ACT.Copy).then_inc(mix_hi, 1)

            def conv():
                for t in range(8):
                    act.wait_ge(S("c_y"), t + 1)
                    a.activation(act2[:, t, 0, :], cy[t % 2][:, :], ACT.Copy).then_inc(mix_hi, 1)

            for l in range(NL):
                u0 = u_layer(l)
                norm(3 + 2 * l)
                for j in range(2):
                    ahead(u0, 0, 2, j)
                if l in (0, 3):
                    a.preload_act_table_set("natural_log_exp_and_others")
                with act.Fori(1, 6) as i:
                    for j in range(2):
                        ahead(u0, i, 2, j)
                ahead(u0 + L_MQ)
                memory_attention(l)
                if l in (0, 3):
                    stick(l // 3)
                elif l == 1:
                    differential()
                else:
                    conv()
                for p in range(4):
                    for j in range(2):
                        ahead(u0 + L_O, p, 2, j)
                    residual(4 + 2 * l, (2 * p, 2 * p + 1))
                swiglu(1 + l, u0 + L_GU, g_gu(l), 4 + 2 * l)
            norm(11)
            for t in range(TT):
                for d in range(2):
                    n = 2 * t + d
                    act.wait_ge(S("out_tr"), n + 1)
                    a.activation(otok[:, t, 512 * d:512 * d + 512], bank(n % 4), ACT.Copy).then_inc(S("out_tile"), 1)

        @block.vector
        def _(dve):
            v = nc.vector
            chain = [0]

            def link(ins):
                chain[0] += 1
                ins.then_inc(S("vec_chain"), 1)
                dve.wait_ge(S("vec_chain"), chain[0])

            def residual(r, wait, src, mode):
                def finish(t):
                    if has_h(r):
                        hn = KD * h_index(r) + t
                        dve.wait_ge(h_hi, hn + 1)
                        if r == 0 and t == 6:
                            dve.wait_ge(S("ext_stored"), 16)
                        v.scalar_tensor_tensor(out=hl[:, t, :], in0=x[:, t, :], scalar=col(gain_col(r) + t),
                                               in1=hh[:, t, :].bitcast(F32), op0=ALU.mult,
                                               op1=ALU.subtract).then_inc(h_ready, 1)

                def add_square(t):
                    n = KD * r + t
                    dve.wait_ge(sq_ready, n + 1)
                    if t == 0:
                        v.tensor_copy(sqacc[:, :], sqb[:, n % 2, :]).then_inc(sq_summed, 1)
                    else:
                        dve.wait_ge(sq_summed, n)
                        v.tensor_tensor(sqacc[:, :], sqacc[:, :], sqb[:, n % 2, :], ALU.add).then_inc(sq_summed, 1)
                for t in range(KD):
                    wait(t)
                    if mode == "copy":
                        ins = v.tensor_copy(x[:, t, :], src(t))
                    elif mode == "add":
                        ins = v.tensor_tensor(x[:, t, :], x[:, t, :], src(t), ALU.add)
                    else:
                        ins = v.scalar_tensor_tensor(out=x[:, t, :], in0=x[:, t, :], scalar=col(C_FIN1 + t),
                                                     in1=rstd[:, :], op0=ALU.mult, op1=ALU.mult)
                    ins.then_inc(x_new, 1)
                    if t:
                        finish(t - 1)
                        if t < KD - 1:
                            add_square(t - 1)
                finish(KD - 1)
                add_square(KD - 2)
                add_square(KD - 1)

            def norm(r, b=6):
                dve.wait_ge(sd_ready, r + 1)
                v.reciprocal(rstdc[:, :], sd[:, :]).then_inc(rstd_ready, 1)
                dve.wait_ge(rstd_ready, 3 * r + 1)
                v.tensor_tensor(sqacc[:, :].rearrange("p (t n) -> p t n", t=TT), bc(ident[:, :], TT),
                                bcl(rstdc[:, :], P), ALU.mult).then_inc(rstd_ready, 1)
                dve.wait_ge(S("rstd_row"), r + 1)
                v.tensor_copy(rstd[:, :], bank(b)).then_inc(rstd_ready, 1)

            def swiglu(s, u0, gc, r):
                def turn(i):
                    def cnt(k, c):
                        return c + k * i if isinstance(i, int) else i * k + c
                    if isinstance(i, int) and i == 0:
                        norm(r, 0)
                        dve.wait_ge(rstd_ready, 3 * (r + 1))
                    dve.wait_ge(unit_used, cnt(2, u0 + 1))
                    v.tensor_tensor(gs[:, :, :], ps[:, 4 * BANK:6 * BANK].rearrange("p (a n) -> p a n", a=2),
                                    bc(rstd[:, :], 2), ALU.mult).then_inc(acc_free, 1)
                    if not isinstance(i, int) or i + s > 0:
                        dve.wait_ge(act_ready, cnt(1, 11 * s))
                    dve.wait_ge(unit_used, cnt(2, u0 + 2))
                    v.tensor_tensor(us[:, :, :], ps[:, 6 * BANK:8 * BANK].rearrange("p (a n) -> p a n", a=2),
                                    bc(rstd[:, :], 2), ALU.mult).then_inc(acc_free, 1)
                    dve.wait_ge(silu_done, cnt(1, 11 * s + 1))
                    dve.wait_ge(acc_free, cnt(2, gc + 2))
                    v.tensor_tensor(us[:, :, :], us[:, :, :], gs[:, :, :], ALU.mult).then_inc(act_step, 1)
                    at_ = 2 * i if isinstance(i, int) else i * 2
                    dve.wait_ge(act_step, cnt(2, 22 * s + 1))
                    v.tensor_scalar(act2[:, bass.ds(at_, 2), 0, :], us[:, :, :], 1.0, None, ALU.mult).then_inc(act_step, 1)
                    dve.wait_ge(act_step, cnt(2, 22 * s + 2))
                    v.tensor_tensor(act2[:, bass.ds(at_, 2), 1, :], us[:, :, :],
                                    act2[:, bass.ds(at_, 2), 0, :].bitcast(F32), ALU.subtract).then_inc(act_ready, 1)
                loop(dve, FF // 256, turn)

            def down_tile(u0, before, t):
                if t % 4 == 3:
                    dve.wait_ge(unit_used, u0 + 6 * (t // 4) + 6)
                else:
                    dve.wait_ge(resid_done, before + 3 * (t // 4) + t % 4 + 1)

            dve.wait_ge(const_ready, 5)
            v.tensor_copy(negtri[:, :], cst[:, :]).then_inc(S("const_r"), 1)
            v.memset(sqacc[:, 0:P], -1.0).then_inc(S("const_r"), 1)
            dve.wait_ge(S("const_r"), 2)
            v.tensor_copy(negones[:, :], sqacc[:, 0:P]).then_inc(S("const_r"), 1)
            dve.wait_ge(S("ssm_loaded"), 48)
            for gi in range(2):
                ins = v.tensor_copy(rows_s[0:ST, 2, NS * gi:NS * gi + NS], ldt[0:ST, gi:gi + 1].broadcast_to([ST, NS]))
            ins.then_inc(S("rows_s_ready"), 1)
            dve.wait_ge(S("ssp_tr"), 1)
            v.tensor_copy(ssp[:, :, :], bank(1, 48).rearrange("p (r i) -> p r i", r=3)).then_inc(S("ssp_ready"), 1)
            pr = lambda k: prep[:, k, :]
            dve.wait_ge(S("dt_ready"), 1)
            v.tensor_tensor(pr(0), ssp[:, 0, :], ssp[:, 2, :], ALU.mult).then_inc(S("a_ready"), 1)
            link(v.tensor_tensor(pr(1), ssp[:, 1, :], ssp[:, 2, :], ALU.mult))
            RND = 1.5 * 2.0 ** 23
            link(v.tensor_scalar(pr(2), pr(1), 1.0 / (2 * math.pi), RND, ALU.mult, ALU.add))
            link(v.tensor_scalar(pr(2), pr(2), RND, None, ALU.subtract))
            c1, c2 = 6.28125, 0.00193500518798828125
            c3 = 2 * math.pi - c1 - c2
            for c in (c1, c2, c3):
                link(v.scalar_tensor_tensor(out=pr(1), in0=pr(2), scalar=-c, in1=pr(1), op0=ALU.mult, op1=ALU.add))
            link(v.tensor_scalar(pr(3), pr(1), 0.125, None, ALU.mult))
            link(v.tensor_tensor(pr(4), pr(3), pr(3), ALU.mult))
            link(v.tensor_scalar(pr(5), pr(4), 1 / 362880.0, -1 / 5040.0, ALU.mult, ALU.add))
            for c in (1 / 120.0, -1 / 6.0, 1.0):
                link(v.tensor_tensor(pr(5), pr(5), pr(4), ALU.mult))
                link(v.tensor_scalar(pr(5), pr(5), c, None, ALU.add))
            link(v.tensor_tensor(pr(5), pr(5), pr(3), ALU.mult))
            link(v.tensor_scalar(pr(6), pr(4), -1 / 40320.0, 1 / 720.0, ALU.mult, ALU.add))
            for c in (-1 / 24.0, 0.5):
                link(v.tensor_tensor(pr(6), pr(6), pr(4), ALU.mult))
                link(v.tensor_scalar(pr(6), pr(6), c, None, ALU.add))
            link(v.tensor_tensor(pr(6), pr(6), pr(4), ALU.mult))
            for _ in range(3):
                link(v.tensor_tensor(pr(7), pr(5), pr(6), ALU.mult))
                link(v.tensor_tensor(pr(8), pr(5), pr(5), ALU.mult))
                link(v.tensor_tensor(pr(7), pr(5), pr(7), ALU.subtract))
                link(v.tensor_scalar(pr(5), pr(7), 2.0, None, ALU.mult))
                link(v.tensor_scalar(pr(6), pr(8), 2.0, None, ALU.mult))
            link(v.tensor_scalar(pr(7), pr(6), -1.0, 1.0, ALU.mult, ALU.add))
            dve.wait_ge(S("small_loaded"), 16 * n_small[0])
            v.tensor_copy(ext[0:NH1, 0:383], ext[0:NH1, 383:384].broadcast_to([NH1, 383])).then_inc(S("rows_ready"), 1)
            dve.wait_ge(S("small_tr"), 1)
            link(v.tensor_copy(cols[:, 0:C_END], bank(0, C_END)))
            link(v.tensor_copy(cols[:, C_CONV:C_CONV + 24], bank(0, 24, P)))
            v.tensor_scalar(gdiff[:, :], col(C_DIFF, 2), 1.0 - LAMBDA_INIT, None, ALU.mult).then_inc(S("cols_ready"), 1)

            dve.wait_ge(const_ready, 5)
            for r in range(2):
                for c in range(4):
                    src = ps[:, (2 + r) * BANK + P * c:(2 + r) * BANK + P * c + P].rearrange("p (j g h) -> p j g h", j=4, g=2)
                    for gi in range(2):
                        rows = slice(NS * gi, NS * gi + NS)
                        v.tensor_scalar(ct[rows, 4 * c:4 * c + 4, r, HG * gi:HG * gi + HG], src[rows, :, gi, :],
                                        -1.0 if r else 1.0, None, ALU.mult).then_inc(S("ct_ready"), 1)

            residual(0, lambda t: dve.wait_ge(S("x_tr"), t + 1), lambda t: bank(4 + t % 4), "copy")

            link(v.memset(er[:, :, 0:1], 1.0))
            link(v.memset(ei[:, :, 0:1], 0.0))
            link(v.tensor_copy(pr(16), pr(7)))
            link(v.tensor_copy(pr(17), pr(5)))

            def double(n, part):
                i0 = 4 * part
                c, s = (bcl(pr(k)[:, i0:i0 + 4], n) for k in (16, 17))
                lo_r, lo_i = er[:, i0:i0 + 4, 0:n], ei[:, i0:i0 + 4, 0:n]
                hi_r, hi_i = er[:, i0:i0 + 4, n:2 * n], ei[:, i0:i0 + 4, n:2 * n]
                s1 = DT[:, 0:4 * n].rearrange("p (i n) -> p i n", i=4)
                s2 = DT[:, 1024:1024 + 4 * n].rearrange("p (i n) -> p i n", i=4)
                v.tensor_tensor(s1, lo_i, s, ALU.mult)
                v.tensor_tensor(s2, lo_r, s, ALU.mult)
                v.tensor_tensor(hi_r, lo_r, c, ALU.mult)
                link(v.tensor_tensor(hi_i, lo_i, c, ALU.mult))
                v.tensor_tensor(hi_r, hi_r, s1, ALU.subtract)
                link(v.tensor_tensor(hi_i, hi_i, s2, ALU.add))
                if part == 3 and n < 256:
                    link(v.tensor_tensor(pr(18), pr(16), pr(16), ALU.mult))
                    link(v.tensor_tensor(pr(19), pr(17), pr(17), ALU.mult))
                    link(v.tensor_tensor(pr(17), pr(16), pr(17), ALU.mult))
                    link(v.tensor_scalar(pr(17), pr(17), 2.0, None, ALU.mult))
                    link(v.tensor_tensor(pr(16), pr(18), pr(19), ALU.subtract))
            DT = at("dtmp", KV0 + 8192, [P, 2048])
            steps = [(1 << e, part) for e in range(9) for part in range(4)]

            norm(0)
            dve.wait_ge(rstd_ready, 3)

            def out_pair(g, dst, scale=1.0):
                src = ps[:, 2 * BANK * (g % 2):2 * BANK * (g % 2) + 2 * BANK].rearrange("p (a n) -> p a n", a=2)
                v.scalar_tensor_tensor(out=dst, in0=src, scalar=scale, in1=bc(rstd[:, :], 2),
                                       op0=ALU.mult, op1=ALU.mult).then_inc(acc_free, 1)

            def out_tokens(par, dst):
                src = ps[:, 2 * BANK * par:2 * BANK * par + 2 * BANK].rearrange("p (t n) -> p t n", t=TT)
                v.tensor_tensor(dst, src, bcl(rstdc[:, :], 256), ALU.mult).then_inc(acc_free, 1)

            def input_matrix():
                dve.wait_ge(S("rmod_ready"), 1)
                link(v.tensor_tensor(pr(9), rmod[:, :], pr(7), ALU.mult))
                link(v.tensor_scalar(pr(9), pr(9), -1.0, None, ALU.add))
                link(v.tensor_tensor(pr(10), rmod[:, :], pr(5), ALU.mult))
                link(v.tensor_tensor(pr(11), ssp[:, 0, :], ssp[:, 0, :], ALU.mult))
                link(v.tensor_tensor(pr(12), ssp[:, 1, :], ssp[:, 1, :], ALU.mult))
                link(v.tensor_tensor(pr(11), pr(11), pr(12), ALU.add))
                link(v.reciprocal(pr(11), pr(11)))
                link(v.tensor_tensor(pr(12), pr(9), ssp[:, 0, :], ALU.mult))
                link(v.tensor_tensor(pr(13), pr(10), ssp[:, 1, :], ALU.mult))
                link(v.tensor_tensor(pr(12), pr(12), pr(13), ALU.add))
                link(v.tensor_tensor(pr(12), pr(12), pr(11), ALU.mult))
                link(v.tensor_tensor(pr(13), pr(10), ssp[:, 0, :], ALU.mult))
                link(v.tensor_tensor(pr(14), pr(9), ssp[:, 1, :], ALU.mult))
                link(v.tensor_tensor(pr(13), pr(13), pr(14), ALU.subtract))
                link(v.tensor_tensor(pr(13), pr(13), pr(11), ALU.mult))
                t1 = sqb[:, 0, 0:ST * HG].rearrange("p (i h) -> p i h", h=HG)
                t2 = sqb[:, 1, 0:ST * HG].rearrange("p (i h) -> p i h", h=HG)
                for r in range(2):
                    link(v.tensor_tensor(t1, braw[:, r, :, :], bcl(pr(12), HG), ALU.mult))
                    link(v.tensor_tensor(t2, braw[:, 1 - r, :, :], bcl(pr(13), HG), ALU.mult))
                    for gi in range(2):
                        rows = slice(NS * gi, NS * gi + NS)
                        v.tensor_tensor(bpre[rows, r, :, HG * gi:HG * gi + HG], t1[rows], t2[rows],
                                        ALU.add if r else ALU.subtract).then_inc(S("bpre_ready"), 1)
                    dve.wait_ge(S("bpre_ready"), 2 * (r + 1))

            def table_steps(u):
                lo, hi = 512 * (u - 2) // 6, 512 * (u - 1) // 6
                for nn, part in steps:
                    if lo < nn * (part + 1) // 4 + nn <= hi:
                        double(nn, part)

            for u in range(8):
                if u == 2:
                    input_matrix()
                table_steps(u)
                if u == 5:
                    dve.wait_ge(S("bt_tr"), 1)
                    for r in range(2):
                        v.tensor_copy(bt[:, :, r, :], bank(4 + r).rearrange("p (c n) -> p c n", c=4)).then_inc(S("bt_ready"), 1)
                dve.wait_ge(unit_used, u + 1)
                if u < 6:
                    out_pair(u, (yu, q1, k1)[u // 2][:, 2 * (u % 2):2 * (u % 2) + 2, :])
                else:
                    out_tokens(u % 2, v1[:, :, 256 * (u % 2):256 * (u % 2) + 256])

            for b in bsb:
                v.memset(b[0:64, 448:512], NEG).then_inc(S("a1_corner"), 1)

            for t in range(NH1 + 2):
                if 1 <= t <= NH1:
                    h = t - 1
                    dve.wait_ge(S("a1_exp"), 4 * t)
                    link(v.reciprocal(rec[:, h % 2, :], sums[:, h % 2, :]))
                    for i in range(4):
                        z = pbuf[h % 2][:, ZQ[i]:ZQ[i] + wq(i)]
                        v.tensor_scalar(z, z, rec[:, h % 2, i:i + 1], None, ALU.mult).then_inc(S("a1_p"), 1)
                if t < NH1:
                    h = t
                    dve.wait_ge(S("a1_z"), h + 1)
                    dve.wait_ge(S("a1_bcopy"), 2 * h + 2)
                    dve.wait_ge(S("a1_corner"), 2)
                    if h >= 2:
                        dve.wait_ge(S("a1_tr"), h - 1)
                    for i in range(4):
                        v.scalar_tensor_tensor(out=pbuf[h % 2][:, ZQ[i]:ZQ[i] + wq(i)],
                                               in0=ps[:, ZQ[i]:ZQ[i] + wq(i)], scalar=DH1 ** -0.5,
                                               in1=bsb[h % 2][:, T - wq(i):T], op0=ALU.mult, op1=ALU.add).then_inc(S("a1_s"), 1)
                    for i in range(4):
                        dve.wait_ge(S("a1_s"), 4 * h + i + 1)
                        v.tensor_reduce(mx[:, h % 2, i:i + 1], pbuf[h % 2][:, ZQ[i]:ZQ[i] + wq(i)], AX.X, ALU.max).then_inc(S("a1_mx"), 1)
                    dve.wait_ge(S("a1_mx"), 4 * (h + 1))
                    v.tensor_scalar(ngm[:, h % 2, :], mx[:, h % 2, :], -1.0, None, ALU.mult).then_inc(S("a1_ngm"), 1)
                if t >= 2 and t % 2 == 1:
                    f = (t - 2) // 2
                    dve.wait_ge(S("a1_pv"), 2 * f + 2)
                    v.tensor_copy(ya[:, f, :], bank(6)).then_inc(S("ya_ready"), 1)

            def back(i):
                dve.wait_ge(S("ssm_x"), 2 * i + 2)
                if i:
                    dve.wait_ge(S("ssm_n"), 4 * i)
                for c in range(2):
                    v.tensor_tensor_scan(out=ss[c][:, :], data0=rmod[:, i:i + 1].broadcast_to([P, T]), data1=sx[c][:, :],
                                         initial=0.0, op0=ALU.mult, op1=ALU.add).then_inc(S("ssm_scan"), 1)
                dve.wait_ge(S("ssm_scan"), 2 * i + 2)
                if i:
                    dve.wait_ge(S("ssm_y"), 2 * i)
                for n, (c, e) in enumerate(((0, er), (1, ei), (0, ei), (1, er))):
                    v.tensor_tensor(sn[n][:, :], ss[c][:, :], e[:, i, :], ALU.mult).then_inc(S("ssm_n"), 1)

            for i in range(ST + 1):
                if i < ST:
                    dve.wait_ge(S("ssm_bu"), i + 1)
                    if i:
                        dve.wait_ge(S("ssm_x"), 2 * i)
                    for n, (c, e) in enumerate(((0, er), (1, ei), (1, er), (0, ei))):
                        v.tensor_tensor(sm[n][:, :], bank(2 * (i % 2) + c), e[:, i, :], ALU.mult).then_inc(S("ssm_m"), 1)
                if i:
                    back(i - 1)
            for c in range(4):
                dve.wait_ge(S("ssm_yd"), 4 * c + 4)
                v.scalar_tensor_tensor(out=yu[:, c, :], in0=yu[:, c, :], scalar=col(C_D + c), in1=bank(4 + c),
                                       op0=ALU.mult, op1=ALU.add).then_inc(S("ssm_skip"), 1)
            for c in range(4):
                dve.wait_ge(S("gelu_hi"), c + 1)
                v.tensor_tensor(gl[:, c, :], yu[:, c, :], gh[:, c, :].bitcast(F32), ALU.subtract).then_inc(S("gelu_lo"), 1)

            def half_norm(n, src, g, slot0):
                for c in range(4):
                    m = 4 * n + c
                    if n == 1:
                        dve.wait_ge(S("sig"), c + 1)
                        v.tensor_tensor(src[:, c, :], src[:, c, :], sig[:, c, :], ALU.mult).then_inc(S("y_gated"), 1)
                    dve.wait_ge(S("hn_sq"), m + 1)
                    if c == 0:
                        v.tensor_copy(sqacc[:, :], sqb[:, m % 2, :]).then_inc(S("hn_sum"), 1)
                    else:
                        dve.wait_ge(S("hn_sum"), m)
                        v.tensor_tensor(sqacc[:, :], sqacc[:, :], sqb[:, m % 2, :], ALU.add).then_inc(S("hn_sum"), 1)
                dve.wait_ge(S("hn_sd"), n + 1)
                link(v.reciprocal(rstd[:, :], rstd[:, :]))
                for c in range(4):
                    v.scalar_tensor_tensor(out=src[:, c, :], in0=src[:, c, :], scalar=col(g + c), in1=rstd[:, :],
                                           op0=ALU.mult, op1=ALU.mult).then_inc(S("hn_y"), 1)
                for c in range(4):
                    m = 4 * n + c
                    dve.wait_ge(mix_hi, m + 1)
                    v.tensor_tensor(act2[:, slot0 + c, 1, :], src[:, c, :], act2[:, slot0 + c, 0, :].bitcast(F32),
                                    ALU.subtract).then_inc(mix_ready, 1)
            half_norm(0, ya, C_ATT, 4)
            half_norm(1, yu, C_SSM, 0)

            residual(1, lambda t: dve.wait_ge(unit_used, U_OUT1 + t // 2 + 1) if t % 2 else dve.wait_ge(resid_done, t // 2 + 1), lambda t: bank((4 + t) % 8), "add")
            swiglu(0, U_GU1, G_GU1, 1)
            dve.wait_ge(S("mem_sd"), 1)
            link(v.reciprocal(rec[:, 1, 0:2], rec[:, 0, 0:2]))
            for t in range(2):
                v.tensor_scalar(mtok[:, t, :], mtok[:, t, :], rec[:, 1, t:t + 1], None, ALU.mult).then_inc(S("mem_scaled"), 1)
            residual(2, lambda t: down_tile(U_DN1, 4, t), lambda t: bank(t), "add")
            for k in range(KD):
                dve.wait_ge(S("mem_hi"), k + 1)
                v.scalar_tensor_tensor(out=ml[:, k, :], in0=bank(k, MEM), scalar=col(C_MEM + k),
                                       in1=mh[:, k, :].bitcast(F32), op0=ALU.mult, op1=ALU.subtract).then_inc(S("mem_ready"), 1)
            norm(2)
            dve.wait_ge(rstd_ready, 9)
            residual(3, lambda t: None, lambda t: None, "norm")
            def kv_turn(i):
                for j in range(2):
                    dve.wait_ge(unit_used, U_KV + 2 * i + j + 1 if isinstance(i, int) else i * 2 + (U_KV + j + 1))
                    src = ps[:, 2 * BANK * j:2 * BANK * j + 2 * BANK].rearrange("p (a n) -> p a n", a=2)[:, :, 0:MEM]
                    dst = (km, vm)[j][:, bass.ds(i, 1), :, :].rearrange("p o a n -> p (o a) n")
                    v.tensor_scalar(dst, src, 1.0, None, ALU.mult).then_inc(acc_free, 1)
            loop(dve, NL, kv_turn, peel=0)

            def mix_low(slot, src, n):
                dve.wait_ge(mix_hi, n + 1)
                v.tensor_tensor(act2[:, slot, 1, :], src, act2[:, slot, 0, :].bitcast(F32), ALU.subtract).then_inc(mix_ready, 1)

            def memory_attention(l, m0):
                def finish(h):
                    n = MH * l + h
                    dve.wait_ge(S("m_exp"), 4 * (n + 1))
                    link(v.reciprocal(rec[:, h % 2, :], sums[:, h % 2, :]))
                    v.tensor_tensor(mp[h % 2][:, :, :], mp[h % 2][:, :, :], bcl(rec[:, h % 2, :], MEM), ALU.mult).then_inc(S("m_p"), 1)
                for h in range(MH + 1):
                    n = MH * l + h
                    if h < MH:
                        dve.wait_ge(S("m_z"), n + 1)
                        src = ps[:, 1024 * (h % 2):1024 * (h % 2) + 1024].rearrange("p (i n) -> p i n", i=4)
                        link(v.tensor_reduce(mx[:, h % 2, :], src, AX.X, ALU.max))
                        v.tensor_scalar(ngm[:, h % 2, :], mx[:, h % 2, :], -(MD ** -0.5), None, ALU.mult).then_inc(S("m_ngm"), 1)
                    if h:
                        finish(h - 1)
                for f in range(2):
                    mix_low(8 + f, bank(6 + f), m0 + f)

            def stick(idx, m0):
                for t in range(NH2 + 2):
                    n = NH2 * idx + t
                    if 1 <= t <= NH2:
                        z = ps[:, 3 * BANK * ((t - 1) % 2):3 * BANK * ((t - 1) % 2) + 3 * BANK]
                        dve.wait_ge(S("k_cum"), n)
                        z3 = z.rearrange("p (b n) -> p b n", b=3)[:, :, 0:P]
                        v.tensor_tensor(z3, z3, bc(cap[:, :], 3), ALU.min).then_inc(S("k_cap"), 1)
                        v.tensor_tensor(z[:, ZK[3]:ZK[3] + P], z[:, ZK[3]:ZK[3] + P], cap[:, :], ALU.min).then_inc(S("k_cap"), 1)
                    if t < NH2:
                        z = ps[:, 3 * BANK * (t % 2):3 * BANK * (t % 2) + ZW]
                        dve.wait_ge(S("k_e"), 3 * (n + 1))
                        if t:
                            dve.wait_ge(S("k_uh"), n)
                        v.scalar_tensor_tensor(out=zu[:, :], in0=z, scalar=0.0, in1=ze[:, :], op0=ALU.max,
                                               op1=ALU.add).then_inc(S("k_u"), 1)
                        dve.wait_ge(S("k_u"), 3 * n + 1)
                        u2 = zu[:, 0:1024].rearrange("p (b n) -> p b n", b=2)[:, :, 0:P]
                        v.tensor_tensor(u2, u2, bc(mask[:, :], 2), ALU.mult).then_inc(S("k_u"), 1)
                        u3 = zu[:, ZK[3]:ZK[3] + 2 * P].rearrange("p (b n) -> p b n", b=2)
                        v.tensor_tensor(u3, u3, bc(mask[:, :], 2), ALU.mult).then_inc(S("k_u"), 1)
                        dve.wait_ge(S("k_uh"), n + 1)
                        v.tensor_tensor(ul[t % 2][:, :], zu[:, :], uh[t % 2][:, :].bitcast(F32), ALU.subtract).then_inc(S("k_ul"), 1)
                    if t >= 2:
                        mix_low(t - 2, bank(6 + t % 2), m0 + 2 + t - 2)

            def differential(m0):
                for c in range(2):
                    v.tensor_tensor(lam[:, c:c + 1], col(C_LAM + 2 * c), col(C_LAM + 2 * c + 1), ALU.mult).then_inc(S("d_lam"), 1)
                dve.wait_ge(S("d_lamexp"), 1)
                link(v.tensor_tensor(lam[:, 4:5], lam[:, 3:4], lam[:, 2:3], ALU.subtract))
                link(v.tensor_scalar(lam[:, 4:5], lam[:, 4:5], -LAMBDA_INIT, None, ALU.add))
                link(v.tensor_reduce(lam[:, 5:6], mask[:, :], AX.X, ALU.add))
                link(v.tensor_scalar(lam[:, 5:6], lam[:, 5:6], -1.0, float(T), ALU.mult, ALU.add))
                link(v.tensor_tensor_scan(out=dist[:, :], data0=ones[:, 0:1].broadcast_to([P, T]),
                                          data1=cst[:, 0:1].broadcast_to([P, T]), initial=lam[:, 5:6],
                                          op0=ALU.mult, op1=ALU.add))
                link(v.tensor_scalar(dneg[:, :], dist[:, :], 0.0, NEG, ALU.is_lt, ALU.mult))
                for hd in range(4):
                    slope = 2.0 ** (-8.0 * (hd + 1) / 4)
                    link(v.scalar_tensor_tensor(out=dbias[:, :], in0=dist[:, :], scalar=-slope, in1=dneg[:, :],
                                                op0=ALU.mult, op1=ALU.add))
                    for c in range(2):
                        m = 2 * hd + c
                        dve.wait_ge(S("d_z"), m + 1)
                        for i in range(4):
                            v.tensor_tensor(pbuf[c][:, ZQ[i]:ZQ[i] + wq(i)], ps[:, ZQ[i]:ZQ[i] + wq(i)],
                                            dbias[:, T - wq(i):T], ALU.add).then_inc(S("d_s"), 1)
                        for i in range(4):
                            dve.wait_ge(S("d_s"), 4 * m + i + 1)
                            v.tensor_reduce(mx[:, c, i:i + 1], pbuf[c][:, ZQ[i]:ZQ[i] + wq(i)], AX.X, ALU.max).then_inc(S("d_mx"), 1)
                        dve.wait_ge(S("d_mx"), 4 * (m + 1))
                        v.tensor_scalar(ngm[:, c, :], mx[:, c, :], -1.0, None, ALU.mult).then_inc(S("d_ngm"), 1)
                    for c in range(2):
                        dve.wait_ge(S("d_exp"), 4 * (2 * hd + c + 1))
                        link(v.reciprocal(rec[:, c, :], sums[:, c, :]))
                    link(v.tensor_scalar(rec[:, 1, :], rec[:, 1, :], lam[:, 4:5], None, ALU.mult))
                    for i in range(4):
                        z = pbuf[0][:, ZQ[i]:ZQ[i] + wq(i)]
                        v.tensor_scalar(z, z, rec[:, 0, i:i + 1], None, ALU.mult).then_inc(S("d_p"), 1)
                    for i in range(4):
                        z = slice(ZQ[i], ZQ[i] + wq(i))
                        dve.wait_ge(S("d_p"), 8 * hd + i + 1)
                        v.scalar_tensor_tensor(out=pbuf[0][:, z], in0=pbuf[1][:, z], scalar=rec[:, 1, i:i + 1],
                                               in1=pbuf[0][:, z], op0=ALU.mult, op1=ALU.add).then_inc(S("d_p"), 1)
                        if i == 3:
                            dve.wait_ge(S("d_p"), 8 * hd + 8)
                    dve.wait_ge(S("d_sd"), hd + 1)
                    link(v.reciprocal(ors[:, :], ors[:, :]))
                    for d in range(2):
                        v.scalar_tensor_tensor(out=us[:, d, :], in0=bank(6 + d), scalar=gdiff[:, d:d + 1], in1=ors[:, :],
                                               op0=ALU.mult, op1=ALU.mult).then_inc(S("d_on"), 1)
                    for d in range(2):
                        mix_low(2 * hd + d, us[:, d, :], m0 + 2 + 2 * hd + d)

            def conv(m0):
                link(v.memset(cv[:, 0:2], 0.0))
                for t in range(8):
                    link(v.tensor_tensor(cv[:, 2:T + 2], k2[:, t, :], vf[:, t, :], ALU.mult))
                    y = cy[t % 2][:, :]
                    if t >= 2:
                        dve.wait_ge(mix_hi, m0 + 2 + t - 1)
                    link(v.tensor_scalar(y, cv[:, 2:T + 2], col(C_CONV + 16 + t), None, ALU.mult))
                    link(v.scalar_tensor_tensor(out=y, in0=cv[:, 1:T + 1], scalar=col(C_CONV + 8 + t), in1=y,
                                                op0=ALU.mult, op1=ALU.add))
                    link(v.scalar_tensor_tensor(out=y, in0=cv[:, 0:T], scalar=col(C_CONV + t), in1=y,
                                                op0=ALU.mult, op1=ALU.add))
                    v.tensor_tensor(y, y, q2[:, t, :], ALU.mult).then_inc(S("c_y"), 1)
                    mix_low(t, y, m0 + 2 + t)

            for l in range(NL):
                u0 = u_layer(l)
                norm(3 + 2 * l)
                dve.wait_ge(rstd_ready, 3 * (4 + 2 * l))
                scale = 1.0 if l == 2 else DH2 ** -0.5

                def qk_turn(i, dst, g, sc):
                    for j in range(2):
                        dve.wait_ge(unit_used, g + 2 * i + j + 1 if isinstance(i, int) else i * 2 + (g + j + 1))
                        at_ = 4 * i + 2 * j if isinstance(i, int) else i * 4 + 2 * j
                        out_pair(j, dst[:, bass.ds(at_, 2), :], sc)
                loop(dve, 2, lambda i: qk_turn(i, q2, u0, scale), peel=0)
                loop(dve, 2, lambda i: qk_turn(i, k2, u0 + 4, 1.0), peel=0)
                if l == 2:
                    loop(dve, 2, lambda i: qk_turn(i, vf, u0 + L_V, 1.0), peel=0)
                else:
                    with dve.Fori(0, 2) as i:
                        for j in range(2):
                            dve.wait_ge(unit_used, i * 2 + (u0 + L_V + j + 1))
                            out_tokens(j, v2[:, :, bass.ds(i * 512 + 256 * j, 256)])
                dve.wait_ge(unit_used, u0 + L_O)
                out_pair(0, mq[:, :, :])
                m0 = 8 + 10 * l
                memory_attention(l, m0)
                if l in (0, 3):
                    stick(l // 3, m0)
                elif l == 1:
                    differential(m0)
                else:
                    conv(m0)
                r = 4 + 2 * l
                residual(r, lambda t: dve.wait_ge(unit_used, u0 + L_O + 2 * (t // 2) + 2) if t % 2 else dve.wait_ge(resid_done, 10 * (l + 1) + t // 2 + 1), lambda t: bank((4 + t) % 8), "add")
                swiglu(1 + l, u0 + L_GU, g_gu(l), r)
                residual(r + 1, lambda t: down_tile(u0 + L_DN, 10 * (l + 1) + 4, t), lambda t: bank(t), "add")
            norm(11)
            dve.wait_ge(rstd_ready, 36)
            for t in range(KD):
                v.scalar_tensor_tensor(out=x[:, t, :], in0=x[:, t, :], scalar=col(C_FIN2 + t), in1=rstd[:, :],
                                       op0=ALU.mult, op1=ALU.mult).then_inc(S("out_scaled"), 1)

        @block.tensor
        def _(pe):
            mm, tr = nc.tensor.matmul, nc.tensor.transpose

            def three(dst, wh, wl, xh, xl, first, last):
                mm(dst, wh, xh, start=first, stop=False, skip_group_check=True)
                mm(dst, wh, xl, start=False, stop=False, skip_group_check=True)
                return mm(dst, wl, xh, start=False, stop=last, skip_group_check=True)

            def unit_ready(u, i=0, per=0):
                pe.wait_ge(lo_made, u + 1 + per * i if isinstance(i, int) else i * per + (u + 1))

            def feature_tiles(slot, banks, xh, xl, kn=KD, n=2, k0=0, first=True, last=True, gate=None, outer_k=True, ks=None):
                ends = {}
                ks = range(kn) if ks is None else ks
                order = [(k, c) for k in ks for c in range(n)] if outer_k else [(k, c) for c in range(n) for k in ks]
                for k, c in order:
                    if gate is not None and c == 0:
                        gate(k)
                    w = slice(k * P * n + P * c, k * P * n + P * c + P)
                    ends[c] = three(banks(c), whi[:, slot, w], wlo[:, slot, w], xh(k0 + k), xl(k0 + k),
                                    first and k == 0, last and k == kn - 1)
                return ends

            def token_tiles(slot, par, th, tl, n=TT, step=256):
                for t in range(n):
                    dst = ps[:, 2 * BANK * par + step * t:2 * BANK * par + step * t + 256]
                    for k in range(KD):
                        hs, ls = th[:, k, P * t:P * t + P], tl[:, k, P * t:P * t + P]
                        w = slice(256 * k, 256 * k + 256)
                        mm(dst, hs, whi[:, slot, w], start=k == 0, stop=False, skip_group_check=True)
                        mm(dst, ls, whi[:, slot, w], start=False, stop=False, skip_group_check=True)
                        e = mm(dst, hs, wlo[:, slot, w], start=False, stop=k == KD - 1, skip_group_check=True)
                return e

            XH, XL = (lambda k: hh[:, k, :]), (lambda k: hl[:, k, :])
            AH, AL = (lambda k: act2[:, k, 0, :]), (lambda k: act2[:, k, 1, :])

            def norm_sum(r, b=6):
                pe.wait_ge(sq_summed, KD * (r + 1))
                for t in range(TT):
                    e = mm(bank(b + 1, 1, t), sqacc[:, P * t:P * t + P], ones[:, 0:1], start=True, stop=True)
                e.then_inc(ssum_done, 1)

            def norm_row(r, b=6):
                pe.wait_ge(rstd_ready, 3 * r + 2)
                mm(bank(b), ones[:, :], sqacc[:, :], start=True, stop=True).then_inc(S("rstd_row"), 1)

            def first_turn(r, u0, b, nb):
                gate = lambda k: pe.wait_ge(h_ready, KD * h_index(r) + k + 1)
                pe.wait_ge(x_new, KD * r + 4)
                unit_ready(u0)
                feature_tiles(u0 % 2, lambda c: bank(b + c), XH, XL, gate=gate)[1].then_inc(unit_used, 1)
                norm_sum(r, nb)
                unit_ready(u0 + 1)
                for ks in (range(4), range(4, KD)):
                    e = feature_tiles((u0 + 1) % 2, lambda c: bank(b + 2 + c), XH, XL, ks=ks)[1]
                    if ks[0] == 0:
                        norm_row(r, nb)
                e.then_inc(unit_used, 1)

            pe.wait_ge(const_ready, 5)
            pe.wait_ge(S("rows_s_ready"), 1)
            for r in range(3):
                e = tr(bank(1, ST, ST * r), rows_s[0:ST, r, :], ident[0:ST, 0:ST])
            e.then_inc(S("ssp_tr"), 1)
            pe.wait_ge(S("rows_ready"), 1)
            tr(bank(0, C_END), rows_a[0:C_END, :], ident[0:C_END, 0:C_END])
            tr(bank(0, 24, P), rows_b[0:24, :], ident[0:24, 0:24])
            for r in range(2):
                for c in range(4):
                    e = tr(bank(2 + r, P, P * c), craw[:, r, c, :, :].rearrange("p d s -> p (d s)"), ident[:, :])
            e.then_inc(S("small_tr"), 1)
            pe.wait_ge(S("x_loaded"), 16)

            def x_tile(f):
                for t in range(TT):
                    e = tr(bank(4 + f % 4, P, P * t), xtok[:, t, P * f:P * f + P], ident[:, :])
                e.then_inc(S("x_tr"), 1)
            for f in range(KD):
                if f >= 4:
                    pe.wait_ge(x_new, f - 3)
                x_tile(f)
            first_turn(0, 0, 0, 6)
            for u in range(2, 8):
                unit_ready(u)
                pe.wait_ge(acc_free, u - 1)
                if u < 6:
                    e = feature_tiles(u % 2, lambda c: bank(2 * (u % 2) + c), XH, XL)[1]
                else:
                    e = token_tiles(u % 2, u % 2, hh, hl)
                e.then_inc(unit_used, 1)
                if u == 4:
                    pe.wait_ge(S("bpre_ready"), 4)
                    for r in range(2):
                        for c in range(4):
                            e = tr(bank(4 + r, P, P * c), bpre[:, r, 4 * c:4 * c + 4, :].rearrange("p i h -> p (i h)"), ident[:, :])
                    e.then_inc(S("bt_tr"), 1)
            pe.wait_ge(acc_free, 8)
            pe.wait_ge(rstd_ready, 3)
            for t in range(NH1 + 2):
                if t < NH1:
                    h, f, rows = t, t // 2, slice(64 * (t % 2), 64 * (t % 2) + 64)
                    pe.wait_ge(S(f"hankel{h % 2}"), 16 * (h // 2 + 1))
                    if h:
                        pe.wait_ge(S("a1_bcopy"), 2 * h)
                    mm(bank(7), flip[:, :], hank[h % 2][:, :], start=True, stop=True).then_inc(S("a1_bias"), 1)
                    if h:
                        pe.wait_ge(S("a1_s"), 4 * h)
                    for i in (0, 2, 3, 1):
                        e = mm(ps[:, ZQ[i]:ZQ[i] + wq(i)], q1[rows, f, P * i:P * i + P], k1[rows, f, 0:wq(i)],
                               start=i != 2, stop=True, skip_group_check=True)
                    e.then_inc(S("a1_z"), 1)
                if 1 <= t <= NH1:
                    h = t - 1
                    pe.wait_ge(S("a1_p"), 4 * t)
                    if h:
                        pe.wait_ge(S("a1_pt"), h)
                    for j in (0, 1, 3, 2):
                        for i in range(j, 4):
                            o = 3 * BANK + ZK[j] + P * (i - j)
                            e = tr(ps[:, o:o + P], pbuf[h % 2][:, ZQ[i] + P * j:ZQ[i] + P * j + P], ident[:, :])
                    e.then_inc(S("a1_tr"), 1)
                if t >= 2:
                    h = t - 2
                    f, r0 = h // 2, 64 * (h % 2)
                    pe.wait_ge(S("a1_pt"), h + 1)
                    if h >= 2:
                        pe.wait_ge(S("ya_ready"), f)
                    for j in range(4):
                        e = mm(ps[r0:r0 + 64, 6 * BANK + P * j:7 * BANK], v1[:, j, DH1 * h:DH1 * h + DH1],
                               ptb[h % 2][:, ZK[j]:ZK[j] + wk(j)], start=j == 0, stop=j == 3, skip_group_check=True)
                    e.then_inc(S("a1_pv"), 1)
            def y_out(i):
                pe.wait_ge(S("ssm_y"), 2 * i + 2)
                c, j = i // 4, i % 4
                dst = ps[32 * j:32 * j + 32, (4 + c) * BANK:(5 + c) * BANK]
                mm(dst, ct[:, i, 0, :], sy[0][:, :], start=True, stop=False, skip_group_check=True)
                mm(dst, ct[:, i, 1, :], sy[1][:, :], start=False, stop=True, skip_group_check=True).then_inc(S("ssm_yd"), 1)
            pe.wait_ge(S("ya_ready"), 4)
            for i in range(ST + 2):
                if i < ST:
                    c, rows = i // 4, slice(32 * (i % 4), 32 * (i % 4) + 32)
                    if i >= 2:
                        pe.wait_ge(S("ssm_m"), 4 * (i - 1))
                    for r in range(2):
                        e = mm(bank(2 * (i % 2) + r), bt[rows, c, r, :], yu[rows, c, :], start=True, stop=True)
                    e.then_inc(S("ssm_bu"), 1)
                if i >= 2:
                    y_out(i - 2)
            unit_ready(U_GLU)
            pe.wait_ge(S("gelu_lo"), 4)
            for c in range(4):
                for k in range(4):
                    w = slice(512 * k + P * c, 512 * k + P * c + P)
                    e = three(bank(c), whi[:, 0, w], wlo[:, 0, w], gh[:, k, :], gl[:, k, :], k == 0, k == 3)
                e.then_inc(S("glu_done") if c < 3 else unit_used, 1)
            for n in range(2):
                pe.wait_ge(S("hn_sum"), 4 * (n + 1))
                if n:
                    pe.wait_ge(S("hn_sd"), n)
                mm(bank(6), ones[:, :], sqacc[:, :], start=True, stop=True).then_inc(S("hn_ssum"), 1)
            for p in range(4):
                unit_ready(U_OUT1 + p)
                if p == 0:
                    pe.wait_ge(mix_ready, 8)
                ends = feature_tiles((U_OUT1 + p) % 2, lambda c: bank((4 + 2 * p + c) % 8), AH, AL, outer_k=False)
                ends[0].then_inc(resid_done, 1)
                ends[1].then_inc(unit_used, 1)

            def swiglu(s, u0, gc, r):
                first_turn(r, u0, 4, 0)
                with pe.Fori(1, FF // 256) as i:
                    for j in range(2):
                        unit_ready(u0 + j, i, 2)
                        pe.wait_ge(acc_free, i * 2 + (gc + j - 1))
                        feature_tiles((u0 + j) % 2, lambda c: bank(4 + 2 * j + c), XH, XL)[1].then_inc(unit_used, 1)

                def down(i):
                    for j in range(6):
                        slot = (u0 + 22 + j) % 2
                        unit_ready(u0 + 22 + j, i, 6)
                        pe.wait_ge(act_ready, 11 * s + min(2 * j + 2, 11))
                        kn = min(4, KF - 4 * j)
                        base = 2048 * i if isinstance(i, int) else i * 2048
                        ends = feature_tiles(slot, lambda c: ps[:, bass.ds(base + 512 * c, 512)], AH, AL, kn=kn, n=4,
                                             k0=4 * j, first=j == 0, last=j == 5, outer_k=j < 5)
                        if j == 5:
                            for c in range(3):
                                ends[c].then_inc(resid_done, 1)
                        ends[3].then_inc(unit_used, 1)
                pe.wait_ge(rstd_ready, 3 * (r + 1))
                loop(pe, 2, down, peel=0)

            swiglu(0, U_GU1, G_GU1, 1)
            pe.wait_ge(S("mem_scaled"), 2)
            for k in range(KD):
                pe.wait_ge(x_new, 2 * KD + k + 1)
                for t in range(2):
                    e = tr(bank(k, P, P * t), mtok[:, t, P * k:P * k + P], ident[:, :])
                e.then_inc(S("mem_tr"), 1)
            pe.wait_ge(S("mem_ready"), KD)
            norm_sum(2)
            norm_row(2)

            def kv(i):
                for j in range(2):
                    unit_ready(U_KV + j, i, 2)
                    if not (isinstance(i, int) and i == 0):
                        pe.wait_ge(acc_free, G_KV + 2 * i + j - 1 if isinstance(i, int) else i * 2 + (G_KV + j - 1))
                    slot = (U_KV + j) % 2
                    if j == 0:
                        e = feature_tiles(slot, lambda c: bank(c, MEM), lambda k: mh[:, k, :], lambda k: ml[:, k, :])[1]
                    else:
                        e = token_tiles(slot, 1, mh, ml, n=2, step=BANK)
                    e.then_inc(unit_used, 1)
            loop(pe, NL, kv, peel=1)
            pe.wait_ge(acc_free, G_L0)

            def memory_attention(l):
                def z(h):
                    n, f, rows = MH * l + h, h // 2, slice(64 * (h % 2), 64 * (h % 2) + 64)
                    if h >= 2:
                        pe.wait_ge(S("m_exp"), 4 * (n - 1))
                    for i in range(4):
                        o = 1024 * (h % 2) + MEM * i
                        e = mm(ps[:, o:o + MEM], mq[rows, f, P * i:P * i + P], km[rows, l, f, :], start=i % 2 == 0,
                               stop=True, skip_group_check=True)
                    e.then_inc(S("m_z"), 1)

                def t_(h):
                    n = MH * l + h
                    pe.wait_ge(S("m_p"), n + 1)
                    if h:
                        pe.wait_ge(S("m_pt"), n)
                    for j in range(2):
                        for i in range(4):
                            e = tr(bank(4 + j, P, P * i), mp[h % 2][:, i, P * j:P * j + P], ident[:, :])
                    e.then_inc(S("m_tr"), 1)

                def pv(h):
                    n, f, r0 = MH * l + h, h // 2, 64 * (h % 2)
                    pe.wait_ge(S("m_pt"), n + 1)
                    for j in range(2):
                        e = mm(ps[r0:r0 + 64, (6 + f) * BANK:(7 + f) * BANK], vm[:, l, j, MD * h:MD * h + MD],
                               mt[h % 2][:, j, :], start=j == 0, stop=j == 1, skip_group_check=True)
                    e.then_inc(S("m_pv"), 1)
                pe.wait_ge(acc_free, g_in(l) + 13)
                for h in range(MH + 2):
                    if h < MH:
                        z(h)
                    if 1 <= h <= MH:
                        t_(h - 1)
                    if h >= 2:
                        pv(h - 2)

            def stick(l, idx, m0):
                for t in range(NH2 + 2):
                    n = NH2 * idx + t
                    if t < NH2:
                        base = 3 * BANK * (t % 2)
                        if t >= 2:
                            pe.wait_ge(S("k_a"), n - 1)
                        elif t == 0:
                            pe.wait_ge(mix_ready, m0 + 2)
                        for j in (0, 1, 3, 2):
                            e = mm(ps[:, base + ZK[j]:base + ZK[j] + wk(j)], k2[:, t, P * j:P * j + P], q2[:, t, P * j:T],
                                   start=j != 3, stop=True, skip_group_check=True)
                        e.then_inc(S("k_z"), 1)
                    if 1 <= t <= NH2:
                        par, base = (t - 1) % 2, 3 * BANK * ((t - 1) % 2)
                        pe.wait_ge(S("k_ul"), n)
                        for part in (uh[par], ul[par]):
                            for j in range(4):
                                for jj in range(j, 4):
                                    o = base + ZK[j] + P * (jj - j)
                                    e = mm(ps[:, o:o + wk(jj)], negtri[:, :] if jj == j else negones[:, :],
                                           part[:, ZK[jj]:ZK[jj] + wk(jj)], start=False, stop=True, skip_group_check=True)
                        e.then_inc(S("k_cum"), 1)
                    if t >= 2:
                        h = t - 2
                        pe.wait_ge(S("k_a"), n - 1)
                        if h >= 2:
                            pe.wait_ge(mix_ready, m0 + 2 + h - 1)
                        for j in range(4):
                            e = mm(bank(6 + t % 2, T - P * j, P * j), v2[:, j, P * h:P * h + P],
                                   az[h % 2][:, ZK[j]:ZK[j] + wk(j)], start=j == 0, stop=j == 3, skip_group_check=True)
                        e.then_inc(S("k_o"), 1)

            def differential(m0):
                pe.wait_ge(S("d_lam"), 2)
                pe.wait_ge(mix_ready, m0 + 2)
                mm(bank(3, 2), ones[:, :], lam[:, 0:2], start=True, stop=True).then_inc(S("d_lamsum"), 1)
                pe.wait_ge(S("d_lamexp"), 1)
                for hd in range(4):
                    for c in range(2):
                        m = 2 * hd + c
                        if m:
                            pe.wait_ge(S("d_s"), 4 * m)
                        for i in (0, 2, 3, 1):
                            e = mm(ps[:, ZQ[i]:ZQ[i] + wq(i)], q2[:, m, P * i:P * i + P], k2[:, m, 0:wq(i)],
                                   start=i != 2, stop=True, skip_group_check=True)
                        e.then_inc(S("d_z"), 1)
                    pe.wait_ge(S("d_p"), 8 * (hd + 1))
                    for j in (0, 1, 3, 2):
                        for i in range(j, 4):
                            o = 3 * BANK + ZK[j] + P * (i - j)
                            e = tr(ps[:, o:o + P], pbuf[0][:, ZQ[i] + P * j:ZQ[i] + P * j + P], ident[:, :])
                    e.then_inc(S("d_tr"), 1)
                    pe.wait_ge(S("d_pt"), hd + 1)
                    if hd:
                        pe.wait_ge(S("d_on"), 2 * hd)
                    for d in range(2):
                        for j in range(4):
                            e = mm(bank(6 + d, T - P * j, P * j), v2[:, j, 256 * hd + P * d:256 * hd + P * d + P],
                                   ptb[0][:, ZK[j]:ZK[j] + wk(j)], start=j == 0, stop=j == 3, skip_group_check=True)
                    e.then_inc(S("d_pv"), 1)
                    pe.wait_ge(S("d_sq"), 2 * hd + 2)
                    mm(bank(3), ones[:, :], osq[0][:, :], start=True, stop=False)
                    mm(bank(3), ones[:, :], osq[1][:, :], start=False, stop=True).then_inc(S("d_ssum"), 1)
                    pe.wait_ge(S("d_sd"), hd + 1)

            for l in range(NL):
                u0, g0, m0, r = u_layer(l), g_in(l), 8 + 10 * l, 3 + 2 * l
                first_turn(r, u0, 0, 6)
                with pe.Fori(1, 6 if l == 2 else 4) as i:
                    for j in range(2):
                        unit_ready(u0 + j, i, 2)
                        pe.wait_ge(acc_free, i * 2 + (g0 + j - 1))
                        feature_tiles((u0 + j) % 2, lambda c: bank(2 * j + c), XH, XL)[1].then_inc(unit_used, 1)
                if l != 2:
                    with pe.Fori(0, 2) as i:
                        for j in range(2):
                            unit_ready(u0 + L_V + j, i, 2)
                            pe.wait_ge(acc_free, i * 2 + (g0 + 8 + j - 1))
                            e = token_tiles((u0 + L_V + j) % 2, j, hh, hl)
                            e.then_inc(unit_used, 1)
                unit_ready(u0 + L_MQ)
                pe.wait_ge(acc_free, g0 + 11)
                e = feature_tiles((u0 + L_MQ) % 2, lambda c: bank(c), XH, XL)[1]
                e.then_inc(unit_used, 1)
                memory_attention(l)
                if l in (0, 3):
                    stick(l, l // 3, m0)
                elif l == 1:
                    differential(m0)
                pe.wait_ge(mix_ready, m0 + 10)

                def out_proj(half, i):
                    base = 2048 * (1 - half)
                    for j in range(2):
                        unit_ready(u0 + L_O + 4 * half + j, i, 2)
                        ends = feature_tiles((u0 + L_O + j) % 2, lambda c: ps[:, bass.ds(1024 * i + (base + 512 * c) if isinstance(i, int) else i * 1024 + (base + 512 * c), 512)],
                                             AH, AL, kn=5, k0=5 * j, first=j == 0, last=j == 1, outer_k=False)
                        if j:
                            ends[0].then_inc(resid_done, 1)
                        ends[1].then_inc(unit_used, 1)
                for half in range(2):
                    loop(pe, 2, lambda i: out_proj(half, i), peel=0)
                swiglu(1 + l, u0 + L_GU, g_gu(l), 4 + 2 * l)
            norm_sum(11)
            norm_row(11)
            pe.wait_ge(S("out_scaled"), KD)
            for t in range(TT):
                for d in range(2):
                    n = 2 * t + d
                    if n >= 4:
                        pe.wait_ge(S("out_tile"), n - 3)
                    for f in range(4):
                        e = tr(bank(n % 4, P, P * f), x[:, 4 * d + f, P * t:P * t + P], ident[:, :])
                    e.then_inc(S("out_tr"), 1)


_INS = [
    "x", "norm_mix_g", "w_in", "ssm_lam_re", "ssm_lam_im", "ssm_log_dt", "ssm_b_re", "ssm_b_im",
    "ssm_c_re", "ssm_c_im", "ssm_d", "ssm_w_glu", "ssm_b_glu", "attn_rel_bias", "norm_ssm_out_g",
    "norm_att_out_g", "w_out", "norm_ffn_g", "w_gate", "w_up", "w_down", "norm_final_g", "mem_2",
    "g_mix_2", "w_in_2", "w_mem_kv_2", "w_o_2", "g_ffn_2", "w_ffn_in_2", "w_ffn_out_2",
    "lam_q1_2", "lam_k1_2", "lam_q2_2", "lam_k2_2", "g_diff_head_2", "conv_w_2", "g_mem_2", "g_final_2",
]


def kernel(**inputs):
    import numpy as _np
    import concourse.bacc as _bacc
    from concourse import mybir as _mybir
    from concourse.bass_utils import run_bass_kernel_spmd as _run

    nc = _bacc.Bacc("TRN2", target_bir_lowering=False, num_devices=1, dynamic_dma_scratch_size=1024)
    arrays, aps = {}, {}
    for name in _INS:
        a = _np.ascontiguousarray(inputs[name])
        arrays[f"in_{name}"] = a
        aps[name] = nc.dram_tensor(f"in_{name}", a.shape, _mybir.dt.from_np(a.dtype), kind="ExternalInput").ap()
    out = nc.dram_tensor("out_dram", (T, D), _mybir.dt.float32, kind="ExternalOutput").ap()
    ext_dram = nc.dram_tensor("bias_rows", (NH1, 640), _mybir.dt.float32, kind="Internal").ap()
    build(nc, aps, out, ext_dram)
    r = _run(nc, [arrays], core_ids=[0])
    return r.results[0]["out_dram"].reshape(1, T, D)
```

```python
import math
from contextlib import ExitStack

import concourse.bass as bass
from concourse import mybir

F32 = mybir.dt.float32
F32R = mybir.dt.float32r
ALU = mybir.AluOpType
ACT = mybir.ActivationFunctionType
AX = mybir.AxisListType

P = 128
T = 512
TT = T // P
D = 1024
KD = D // P
FF = 2816
KF = FF // P
DS = 512
GRP, HG, NS = 32, 16, 64
ST = GRP * NS // P
NH1, DH1 = 8, 64
MAXREL = 128
NL = 4
NH2, DH2 = 8, 128
MEM, MH, MD = 256, 4, 64
WIN2 = 3 * D + MH * MD
KO = (D + MH * MD) // P
BANK = 512
UNIT = 2048
NEG, BIG = -1e30, 3e38
EPS, HEPS = 1e-6, 1e-5

U_IN1, U_GLU, U_OUT1 = 0, 8, 9
U_GU1 = U_OUT1 + 4
U_DN1 = U_GU1 + 2 * (FF // 256)
U_KV = U_DN1 + 12
U_L0 = U_KV + 2 * NL
L_V, L_O, L_GU, L_DN = 9, 13, 21, 43
PER_LAYER = 55
UNITS = U_L0 + NL * PER_LAYER

ZK = {0: 0, 1: 512, 3: 896, 2: 1024}
ZQ = {0: 0, 2: 128, 3: 512, 1: 1024}
ZW = 1280


def wk(j):
    return T - P * j


def wq(i):
    return P * (i + 1)


C_MIX1, C_FFN1, C_FIN1, C_MIX2, C_FFN2, C_MEM, C_FIN2 = 0, 8, 16, 24, 56, 88, 96
C_SSM, C_ATT, C_BGLU, C_D, C_DIFF, C_LAM, C_END = 104, 108, 112, 116, 120, 122, 126
C_CONV = 126


def has_h(r):
    return r not in (2, 11)


def h_index(r):
    return sum(has_h(q) for q in range(r))


def gain_col(r):
    if r == 0:
        return C_MIX1
    if r == 1:
        return C_FFN1
    if r % 2:
        return C_MIX2 + KD * ((r - 3) // 2)
    return C_FFN2 + KD * ((r - 4) // 2)


def loop(eng, n, body, peel=1):
    for i in range(peel):
        body(i)
    if n > peel:
        with eng.Fori(peel, n) as i:
            body(i)


def build(nc, A, out, ext_dram):
    with ExitStack() as ctx:
        sems = {}

        def S(name):
            if name not in sems:
                sems[name] = ctx.enter_context(nc.semaphore(name))
            return sems[name]

        top = [1152]

        def at(name, offset, shape, dt=F32):
            return nc.alloc_sbuf_tensor_at(name, shape, dt, offset=offset)

        def place(nbytes):
            o = top[0]
            top[0] += (nbytes + 31) // 32 * 32
            return o

        x = at("x", place(KD * T * 4), [P, KD, T])
        H0 = place(2 * KD * T * 4)
        hh = at("hh", H0, [P, KD, T], F32R)
        hl = at("hl", H0 + KD * T * 4, [P, KD, T], F32R)
        A0 = place(KF * 2 * T * 4)
        act2 = at("act2", A0, [P, KF, 2, T], F32R)
        raw = at("raw", place(2 * UNIT * 4), [P, 2, UNIT])
        whi = at("whi", place(2 * UNIT * 4), [P, 2, UNIT], F32R)
        wlo = at("wlo", place(2 * UNIT * 4), [P, 2, UNIT], F32R)
        KV0 = place(2 * NL * 2 * MEM * 4)
        km = at("km", KV0, [P, NL, 2, MEM])
        vm = at("vm", KV0 + NL * 2 * MEM * 4, [P, NL, 2, MEM])
        GS0 = place(2 * T * 4)
        gs = at("gs", GS0, [P, 2, T])
        mq = at("mq", GS0, [P, 2, T])
        US0 = place(2 * T * 4)
        us = at("us", US0, [P, 2, T])
        rstd = at("rstd", place(T * 4), [P, T])
        sqacc = at("sqacc", place(T * 4), [P, T])
        SQB0 = place(2 * T * 4)
        sqb = at("sqb", SQB0, [P, 2, T])
        ident = at("ident", place(P * 4), [P, P])
        ones = at("ones", place(P * 4), [P, P])
        negtri = at("negtri", place(P * 4), [P, P], F32R)
        negones = at("negones", place(P * 4), [P, P], F32R)
        mask = at("mask", place(P * 4), [P, P])
        cap = at("cap", place(P * 4), [P, P])
        cols = at("cols", place(152 * 4), [P, 152])
        rstdc = at("rstdc", place(TT * 4), [P, TT])
        sd = at("sd", place(TT * 4), [P, TT])
        epsc = at("epsc", place(4), [P, 1])
        hepsc = at("hepsc", place(4), [P, 1])
        mx = at("mx", place(32), [P, 2, 4])
        ngm = at("ngm", place(2 * 16), [P, 2, 4])
        sums = at("sums", place(2 * 16), [P, 2, 4])
        rec = at("rec", place(2 * 16), [P, 2, 4])
        lam = at("lam", place(32), [P, 8])
        gdiff = at("gdiff", place(8), [P, 2])
        ssp = at("ssp", place(3 * 64), [P, 3, 16])
        rmod = at("rmod", place(64), [P, ST])
        cst = at("cst", place(P * 4), [P, P])
        flip = at("flip", place(P * 4), [P, P])
        assert top[0] <= 229344, top[0]

        er = at("er", A0, [P, ST, T])
        ei = at("ei", A0 + ST * T * 4, [P, ST, T])
        QKV1 = A0 + 65536
        q1 = at("q1", QKV1, [P, 4, T])
        k1 = at("k1", QKV1 + 8192, [P, 4, T])
        v1 = at("v1", QKV1 + 16384, [P, TT, T])
        xtok = at("xtok", QKV1, [P, TT, D])
        yu = at("yu", KV0, [P, 4, T])
        ya = at("ya", KV0 + 8192, [P, 4, T])
        QKV2 = A0 + 10 * 2 * T * 4
        q2 = at("q2", QKV2, [P, 8, T])
        k2 = at("k2", QKV2 + 16384, [P, 8, T])
        v2 = at("v2", QKV2 + 32768, [P, TT, D])
        vf = at("vf", QKV2 + 32768, [P, 8, T])
        mtok = at("mtok", KV0, [P, 2, D])
        mh = at("mh", A0, [P, KD, MEM], F32R)
        ml = at("ml", A0 + 8192, [P, KD, MEM], F32R)
        otok = at("otok", A0, [P, TT, D])

        ps = ctx.enter_context(nc.psum_tensor("ps", [P, 8 * BANK], F32))

        def bank(b, w=BANK, off=0):
            return ps[:, b * BANK + off:b * BANK + off + w]

        def col(c, n=1):
            return cols[:, c:c + n]

        w_in1 = A["w_in"][0].rearrange("(k p) n -> p k n", p=P)
        w_glu = A["ssm_w_glu"][0].rearrange("(k p) n -> p k n", p=P)
        w_out1 = A["w_out"][0].rearrange("(k p) n -> p k n", p=P)
        w_g1 = A["w_gate"][0].rearrange("(k p) n -> p k n", p=P)
        w_u1 = A["w_up"][0].rearrange("(k p) n -> p k n", p=P)
        w_d1 = A["w_down"][0].rearrange("(k p) n -> p k n", p=P)
        w_in2 = [A["w_in_2"][l].rearrange("(k p) n -> p k n", p=P) for l in range(NL)]
        w_kv2 = [A["w_mem_kv_2"][l].rearrange("(k p) n -> p k n", p=P) for l in range(NL)]
        w_o2 = [A["w_o_2"][l].rearrange("(k p) n -> p k n", p=P) for l in range(NL)]
        w_f2 = [A["w_ffn_in_2"][l].rearrange("(k p) n -> p k n", p=P) for l in range(NL)]
        w_d2 = [A["w_ffn_out_2"][l].rearrange("(k p) n -> p k n", p=P) for l in range(NL)]

        loaded = [S("loaded0"), S("loaded1")]
        hi_made, lo_made, unit_used = S("hi_made"), S("lo_made"), S("unit_used")
        acc_free = S("acc_free")
        resid_done, x_new, h_hi, h_ready = S("resid_done"), S("x_new"), S("h_hi"), S("h_ready")
        sq_ready, sq_summed = S("sq_ready"), S("sq_summed")
        ssum_done, sd_ready, rstd_ready = S("ssum_done"), S("sd_ready"), S("rstd_ready")
        silu_done, act_step, act_ready = S("silu_done"), S("act_step"), S("act_ready")
        mix_hi, mix_ready = S("mix_hi"), S("mix_ready")
        const_step, const_ready = S("const_step"), S("const_ready")


        G_GU1, G_KV, G_L0 = 8, 30, 38

        def g_in(l):
            return G_L0 + 35 * l

        def g_gu(l):
            return g_in(l) + 13

        def u_layer(l):
            return U_L0 + PER_LAYER * l

        def mix_index(l, slot):
            order = (0, 1, 8, 2, 3, 9, 4, 5, 6, 7) if l == 2 else (8, 9, 0, 1, 2, 3, 4, 5, 6, 7)
            return 8 + 10 * l + order.index(slot)

        braw = at("braw", QKV1 + 16384, [P, 2, ST, HG])
        bpre = at("bpre", QKV1 + 16384 + 2048, [P, 2, ST, 32])
        prep = at("prep", place(20 * ST * 4), [P, 20, ST])
        rows_a = at("rows_a", KV0 + 8192, [P, P])
        rows_b = at("rows_b", KV0 + 8192 + 512, [P, P])
        rows_s = at("rows_s", KV0 + 8192 + 1024, [P, 3, P])
        craw = at("craw", KV0 + 8192 + 2560, [P, 2, 4, 2, NS])
        ext = at("ext", GS0, [P, 640])
        ldt = at("ldt", KV0 + 8192 + 6656, [P, 2])
        bt = at("bt", GS0, [P, 4, 2, P])
        ct = at("ct", US0, [P, ST, 2, 32])
        pbuf = [at(f"pbuf{i}", H0 + 5120 * i, [P, ZW]) for i in range(2)]
        ptb = [at(f"ptb{i}", H0 + 10240 + 5120 * i, [P, ZW]) for i in range(2)]
        hank = [at(f"hank{i}", H0 + 20480 + 2048 * i, [P, T]) for i in range(2)]
        hank_early = [at(f"hank_early{i}", KV0 + 12288 + 2048 * i, [P, T]) for i in range(2)]

        def hankel_tile(h):
            return hank_early[h] if h < 2 else hank[h % 2]
        bsb = [at(f"bsb{i}", H0 + 24576 + 2048 * i, [P, T]) for i in range(2)]
        tscr = [at(f"tscr{i}", H0 + 28672 + 2048 * i, [P, T]) for i in range(2)]
        sm = [at(f"sm{i}", H0 + 2048 * i, [P, T]) for i in range(4)]
        sx = [at(f"sx{i}", H0 + 8192 + 2048 * i, [P, T]) for i in range(2)]
        ss = [at(f"ss{i}", H0 + 12288 + 2048 * i, [P, T]) for i in range(2)]
        sn = [at(f"sn{i}", H0 + 16384 + 2048 * i, [P, T]) for i in range(4)]
        sy = [at(f"sy{i}", H0 + 24576 + 2048 * i, [P, T]) for i in range(2)]
        gh = at("gh", H0, [P, 4, T], F32R)
        gl = at("gl", H0 + 8192, [P, 4, T], F32R)
        sig = at("sig", H0 + 16384, [P, 4, T])
        ze = at("ze", H0, [P, ZW])
        zu = at("zu", H0 + 5120, [P, ZW])
        uh = [at(f"uh{i}", H0 + 10240 + 10240 * i, [P, ZW], F32R) for i in range(2)]
        ul = [at(f"ul{i}", H0 + 15360 + 10240 * i, [P, ZW], F32R) for i in range(2)]
        az = [at(f"az{i}", H0 + 10240 + 10240 * i, [P, ZW]) for i in range(2)]
        dp = [at(f"dp{i}", H0 + 5120 * i, [P, ZW]) for i in range(4)]
        dpt = at("dpt", H0 + 20480, [P, ZW])
        osq = [at(f"osq{i}", H0 + 25600 + 2048 * i, [P, T]) for i in range(2)]
        ors = at("ors", H0 + 29696, [P, T])
        dbias = at("dbias", GS0, [P, T])
        dist = at("dist", GS0 + 2048, [P, T])
        dneg = at("dneg", SQB0, [P, T])
        mp = at("mp", A0 + 4 * 2 * T * 4, [P, 4, MEM])
        mt = at("mt", A0 + 5 * 2 * T * 4, [P, 2, T])
        cv = at("cv", SQB0, [P, T + 2])
        cy = [at(f"cy{i}", US0 + 2048 * i, [P, T]) for i in range(2)]

        def bc(ap2, n):
            m = ap2.shape[1]
            return ap2.rearrange("p (a m) -> p a m", a=1).broadcast_to([P, n, m])

        def bcl(ap2, n):
            m = ap2.shape[1]
            return ap2.rearrange("p (m a) -> p m a", a=1).broadcast_to([P, m, n])

        n_small = [0]
        LAMBDA_INIT = 0.8 - 0.6 * math.exp(-0.3)
        block = ctx.enter_context(nc.Block())

        @block.sync
        def _(sp):
            for k, name in ((0, "ssm_lam_re"), (1, "ssm_lam_im")):
                sp.dma_start(rows_s[0:ST, k, :], A[name][0].rearrange("(i g) s -> i (g s)", g=2)).then_inc(S("ssm_loaded"), 16)
            sp.dma_start(ldt[0:ST, :], A["ssm_log_dt"][0].rearrange("(i g) -> i g", g=2)).then_inc(S("ssm_loaded"), 16)
            sp.dma_start(rows_a[C_MIX1:C_MIX1 + 8, :], A["norm_mix_g"][0].rearrange("(t p) -> t p", p=P)).then_inc(S("gain_loaded"), 16)

            def load(slot, kn, cn, src, need):
                dst = raw[:, slot, 0:kn * cn].rearrange("p (k n) -> p k n", n=cn)
                if need is not None:
                    sp.wait_ge(lo_made, need)
                sp.dma_start(dst, src).then_inc(loaded[slot], 16)

            def pair_loop(n, u0, kn, cn, src_of, peel=0, per=2):
                def turn(i):
                    where, need = [], []
                    for j in range(per):
                        w, k0, kk, c0, step = src_of(j)
                        where.append((w, k0, kk, c0 + step * i if isinstance(i, int) else sp.snap(i * step + c0)))
                        u = u0 + j
                        if isinstance(i, int):
                            v = u + per * i - 1
                            need.append(v if v > 0 else None)
                        else:
                            need.append(sp.snap(i * per + (u - 1)))
                    for j in range(per):
                        w, k0, kk, off = where[j]
                        load((u0 + j) % 2, kk, cn, w[:, k0:k0 + kk, bass.ds(off, cn)], need[j])
                loop(sp, n, turn, peel)

            def swiglu(u0, wg, g0, wu, u1, wd, between=None):
                pair_loop(FF // 256, u0, KD, 256, lambda j: ((wg, 0, KD, g0, 256), (wu, 0, KD, u1, 256))[j])
                if between:
                    between()
                pair_loop(2, u0 + 22, 4, 512, lambda j: (wd, 4 * j, min(4, KF - 4 * j), 0, 512), per=6)

            load(0, KD, 256, w_in1[:, :, 0:256], None)
            sp.dma_start(xtok[:, :, :], A["x"][0].rearrange("(t p) d -> p t d", p=P)).then_inc(S("x_loaded"), 16)
            load(1, KD, 256, w_in1[:, :, 256:512], None)

            def small(dst, src):
                n_small[0] += 1
                sp.dma_start(dst, src).then_inc(S("small_loaded"), 16)

            def vec(c, name, n, w=None):
                v = A[name] if w is None else w
                small(rows_a[c:c + n, :], v)
            for c, name, n in ((C_FFN1, "norm_ffn_g", 8),
                               (C_SSM, "norm_ssm_out_g", 4), (C_ATT, "norm_att_out_g", 4),
                               (C_BGLU, "ssm_b_glu", 4), (C_DIFF, "g_diff_head_2", 2)):
                vec(c, name, n, A[name][0].rearrange("(t p) -> t p", p=P))
            for c, name in ((C_FIN1, "norm_final_g"), (C_MEM, "g_mem_2"), (C_FIN2, "g_final_2")):
                vec(c, name, 8, A[name].rearrange("(t p) -> t p", p=P))
            for c, name in ((C_MIX2, "g_mix_2"), (C_FFN2, "g_ffn_2")):
                vec(c, name, 32, A[name].rearrange("l (t p) -> (l t) p", p=P))
            vec(C_D, "ssm_d", 4, A["ssm_d"][0].rearrange("(t g) h -> t (g h)", t=4))
            for i, name in enumerate(("lam_q1_2", "lam_k1_2", "lam_q2_2", "lam_k2_2")):
                vec(C_LAM + i, name, 1, A[name])
            small(rows_b[0:24, :], A["conv_w_2"][0].rearrange("i (t p) -> (i t) p", p=P))
            for r, name in enumerate(("ssm_b_re", "ssm_b_im")):
                small(braw[:, r, :, :], A[name][0].rearrange("(i g) s h -> (g s) i h", g=2))
            for r, name in enumerate(("ssm_c_re", "ssm_c_im")):
                for d in range(2):
                    small(craw[:, r, :, d, :], A[name][0].rearrange("(c g) h s -> (g h) c s", c=4))
            small(ext[0:NH1, 383:639], A["attn_rel_bias"][0][:, 0:256])

            pair_loop(3, U_IN1 + 2, KD, 256, lambda j: (w_in1, 0, KD, 512 + 256 * j, 512), peel=1)
            load(U_GLU % 2, 4, 512, w_glu[:, 0:4, :], U_GLU - 1)
            pair_loop(2, U_OUT1, KD, 256, lambda j: (w_out1, 0, KD, 256 * j, 512))

            def memory():
                sp.wait_ge(S("mix_ready"), 8)
                sp.dma_start(mtok[:, :, :], A["mem_2"][0].rearrange("(t p) d -> p t d", p=P)).then_inc(S("mem_loaded"), 16)
            swiglu(U_GU1, w_g1, 0, w_u1, 0, w_d1, memory)
            for l in range(NL):
                for j in range(2):
                    u = U_KV + 2 * l + j
                    load(u % 2, KD, 256, w_kv2[l][:, :, 256 * j:256 * j + 256], u - 1)
            for l in range(NL):
                u0 = u_layer(l)
                load(u0 % 2, KD, 256, w_in2[l][:, :, 3 * D:3 * D + 256], u0 - 1)
                if l == 2:
                    pair_loop(2, u0 + 1, KD, 256, lambda j: (w_in2[l], 0, KD, D * (j % 3) + 256 * (j // 3), 512), per=6)
                else:
                    pair_loop(6, u0 + 1, KD, 256, lambda j: (w_in2[l], 0, KD, 256 * j, 512))
                pair_loop(4, u0 + L_O, 5, 256, lambda j: (w_o2[l], 5 * j, 5, 0, 256))
                swiglu(u0 + L_GU, w_f2[l], 0, w_f2[l], FF, w_d2[l])
            for t in range(TT):
                sp.wait_ge(S("out_tile"), 2 * (t + 1))
                sp.dma_start(out[P * t:P * t + P, :], otok[:, t, :]).then_inc(S("stored"), 16)
            sp.wait_ge(S("stored"), 16 * TT)

        @block.gpsimd
        def _(pool):
            g = nc.gpsimd
            g.memset(ident[:, :], 0.0).then_inc(const_step, 1)
            g.memset(ones[:, :], 1.0).then_inc(const_step, 1)
            g.memset(flip[:, :], 0.0).then_inc(const_step, 1)
            g.memset(mask[:, :], 1.0).then_inc(const_step, 1)
            g.memset(cap[:, :], BIG).then_inc(const_step, 1)
            g.memset(cst[:, :], -1.0).then_inc(const_step, 1)
            g.memset(epsc[:, :], EPS).then_inc(const_step, 1)
            g.memset(hepsc[:, :], HEPS).then_inc(const_step, 1)
            g.memset(bpre[:, :, :, :], 0.0).then_inc(const_step, 1)
            g.memset(ct[:, :, :, :], 0.0).then_inc(const_step, 1)
            pool.wait_ge(const_step, 10)
            g.affine_select(out=ident[:, :], in_=ident[:, :], compare_op=ALU.not_equal, fill=1.0,
                            base=0, pattern=[[-1, P]], channel_multiplier=1).then_inc(const_ready, 1)
            g.affine_select(out=flip[:, :], in_=flip[:, :], compare_op=ALU.not_equal, fill=1.0,
                            base=-(P - 1), pattern=[[1, P]], channel_multiplier=1).then_inc(const_ready, 1)
            g.affine_select(out=mask[:, :], in_=mask[:, :], compare_op=ALU.is_gt, fill=0.0,
                            base=0, pattern=[[1, P]], channel_multiplier=-1).then_inc(const_ready, 1)
            g.affine_select(out=cap[:, :], in_=cap[:, :], compare_op=ALU.is_gt, fill=NEG,
                            base=0, pattern=[[1, P]], channel_multiplier=-1).then_inc(const_ready, 1)
            g.affine_select(out=cst[:, :], in_=cst[:, :], compare_op=ALU.is_ge, fill=0.0,
                            base=0, pattern=[[-1, P]], channel_multiplier=1).then_inc(const_ready, 1)

            def low(slot, need):
                pool.wait_ge(hi_made, need)
                g.tensor_tensor(wlo[:, slot, :], raw[:, slot, :], whi[:, slot, :].bitcast(F32),
                                ALU.subtract).then_inc(lo_made, 1)

            loop(pool, 5, lambda i: [low(j, 2 * i + j + 1) for j in range(2)], peel=1)
            pool.wait_ge(S("table_half"), 1)
            pool.wait_ge(unit_used, 8)
            h = T // 2
            for n in range(ST // 2):
                tiles = slice(2 * n, 2 * n + 2)
                c, s_ = (bcl(prep[:, k, tiles], h) for k in (16, 17))
                s1, s2 = (b[:, :].rearrange("p (i n) -> p i n", i=2) for b in tscr)
                if n:
                    pool.wait_ge(S("table_high"), 6 * n)
                g.tensor_tensor(s1, ei[:, tiles, 0:h], s_, ALU.mult).then_inc(S("table_high"), 1)
                g.tensor_tensor(s2, er[:, tiles, 0:h], s_, ALU.mult).then_inc(S("table_high"), 1)
                g.tensor_tensor(er[:, tiles, h:T], er[:, tiles, 0:h], c, ALU.mult).then_inc(S("table_high"), 1)
                g.tensor_tensor(ei[:, tiles, h:T], ei[:, tiles, 0:h], c, ALU.mult).then_inc(S("table_high"), 1)
                pool.wait_ge(S("table_high"), 6 * n + 4)
                g.tensor_tensor(er[:, tiles, h:T], er[:, tiles, h:T], s1, ALU.subtract).then_inc(S("table_high"), 1)
                g.tensor_tensor(ei[:, tiles, h:T], ei[:, tiles, h:T], s2, ALU.add).then_inc(S("table_high"), 1)
            for t in range(ST + 1):
                if t < ST:
                    pool.wait_ge(S("ssm_m"), 4 * (t + 1))
                    if t:
                        pool.wait_ge(S("ssm_scan"), 2 * t)
                    g.tensor_tensor(sx[0][:, :], sm[0][:, :], sm[1][:, :], ALU.add).then_inc(S("ssm_x"), 1)
                    g.tensor_tensor(sx[1][:, :], sm[2][:, :], sm[3][:, :], ALU.subtract).then_inc(S("ssm_x"), 1)
                if t:
                    pool.wait_ge(S("ssm_n"), 4 * t)
                    if t > 1:
                        pool.wait_ge(S("ssm_yd"), t - 1)
                    g.tensor_tensor(sy[0][:, :], sn[0][:, :], sn[1][:, :], ALU.subtract).then_inc(S("ssm_y"), 1)
                    g.tensor_tensor(sy[1][:, :], sn[2][:, :], sn[3][:, :], ALU.add).then_inc(S("ssm_y"), 1)
            with pool.Fori(5, UNITS // 2) as i:
                for j in range(2):
                    low(j, i * 2 + (j + 1))
            low(0, UNITS)

        @block.scalar
        def _(act):
            a = nc.scalar

            def high(slot, load_need, used_need):
                act.wait_ge(loaded[slot], load_need)
                if used_need is not None:
                    act.wait_ge(unit_used, used_need)
                a.activation(whi[:, slot, :], raw[:, slot, :], ACT.Copy).then_inc(hi_made, 1)

            def ahead(u0, i=0, per=0, j=0):
                v = u0 + j + 2
                if isinstance(i, int):
                    v += per * i
                    if v < UNITS:
                        high(v % 2, 16 * (v // 2 + 1), v - 1)
                else:
                    high(v % 2, i * (8 * per) + 16 * (v // 2 + 1), i * per + (v - 1))

            def residual(r, tiles=range(KD)):
                for t in tiles:
                    n = KD * r + t
                    act.wait_ge(x_new, n + 1)
                    if has_h(r):
                        a.activation(hh[:, t, :], x[:, t, :], ACT.Identity,
                                     scale=col(gain_col(r) + t)).then_inc(h_hi, 1)
                    if n >= 2:
                        act.wait_ge(sq_summed, n - 1)
                    a.activation(sqb[:, n % 2, :], x[:, t, :], ACT.Square).then_inc(sq_ready, 1)

            def norm(r, b=6):
                act.wait_ge(ssum_done, r + 1)
                a.activation(sd[:, :], bank(b + 1, TT), ACT.Sqrt, bias=epsc[:, :], scale=1.0 / D).then_inc(sd_ready, 1)

            def swiglu(s, u0, gc, r, between=None):
                def turn(i):
                    first = isinstance(i, int) and i == 0
                    if first:
                        norm(r, 0)
                        ahead(u0)
                    act.wait_ge(acc_free, gc + 1 + i * 2 if isinstance(i, int) else i * 2 + (gc + 1))
                    a.activation(gs[:, :, :], gs[:, :, :], ACT.Silu).then_inc(silu_done, 1)
                    for j in range(1 if first else 0, 2):
                        ahead(u0, i, 2, j)
                loop(act, FF // 256, turn)
                for i in range(2):
                    for j in range(6):
                        if 6 * i + j == 11:
                            residual(r + 1, range(4, 7))
                        ahead(u0 + 22, i, 6, j)
                    if i == 0:
                        if between:
                            between()
                        residual(r + 1, range(4))
                residual(r + 1, range(7, 8))

            act.wait_ge(S("ssp_ready"), 1)
            a.activation(ssp[:, 2, :], ssp[:, 2, :], ACT.Exp).then_inc(S("dt_ready"), 1)
            act.wait_ge(S("a_ready"), 1)
            a.activation(rmod[:, :], prep[:, 0, :], ACT.Exp).then_inc(S("rmod_ready"), 1)
            high(0, 16, None)
            act.wait_ge(S("gain_ready"), 1)
            residual(0, range(2))
            high(1, 16, None)
            residual(0, range(2, KD))
            def hankel(h):
                src = bass.AP(tensor=ext_dram.tensor, offset=640 * h, ap=[[1, P], [1, T]])
                act.dma_start(hankel_tile(h)[:, :], src).then_inc(S(f"hankel{h % 2}"), 16)

            norm(0)
            for u in range(8):
                ahead(u)
                if u == 4:
                    act.wait_ge(S("ext_stored"), 16)
                    act.wait_ge(S("small_tr"), 1)
                    hankel(0)
                    hankel(1)
                if u == 2:
                    act.wait_ge(S("rows_ready"), 1)
                    act.dma_start(ext_dram[:, 0:639], ext[0:NH1, 0:639]).then_inc(S("ext_stored"), 16)

            def relcopy(h):
                act.wait_ge(S("a1_bias"), h + 1)
                if h >= 2:
                    act.wait_ge(S("a1_s"), 4 * (h - 1))
                b = bsb[h % 2]
                a.activation(b[:, 0:448], bank(7, 448), ACT.Copy).then_inc(S("a1_bcopy"), 1)
                a.activation(b[64:128, 448:512], ps[64:128, 7 * BANK + 448:8 * BANK], ACT.Copy).then_inc(S("a1_bcopy"), 1)

            for t in range(NH1 + 1):
                if t < NH1:
                    relcopy(t)
                    if t + 2 < NH1:
                        hankel(t + 2)
                    act.wait_ge(S("a1_ngm"), t + 1)
                    for i in range(4):
                        z = pbuf[t % 2][:, ZQ[i]:ZQ[i] + wq(i)]
                        a.activation(z, z, ACT.Exp, bias=ngm[:, t % 2, i:i + 1],
                                     accum_out=sums[:, t % 2, i:i + 1]).then_inc(S("a1_exp"), 1)
                if t:
                    act.wait_ge(S("a1_tr"), t)
                    if t >= 3:
                        act.wait_ge(S("a1_pv"), t - 2)
                    a.activation(ptb[(t - 1) % 2][:, :], ps[:, 3 * BANK:3 * BANK + ZW], ACT.Copy).then_inc(S("a1_pt"), 1)

            def half_square(n, c):
                m = 4 * n + c
                if m >= 2:
                    act.wait_ge(S("hn_sum"), m - 1)
                a.activation(sqb[:, m % 2, :], (ya, yu)[n][:, c, :], ACT.Square).then_inc(S("hn_sq"), 1)

            def half_root(n):
                act.wait_ge(S("hn_ssum"), n + 1)
                a.activation(rstd[:, :], bank(6), ACT.Sqrt, bias=epsc[:, :], scale=1.0 / DS).then_inc(S("hn_sd"), 1)

            def half_high(n):
                for c in range(4):
                    act.wait_ge(S("hn_y"), 4 * n + c + 1)
                    a.activation(act2[:, 4 * (1 - n) + c, 0, :], (ya, yu)[n][:, c, :], ACT.Copy).then_inc(mix_hi, 1)

            for c in range(4):
                act.wait_ge(S("ya_ready"), c + 1)
                half_square(0, c)
            half_root(0)
            for c in range(4):
                act.wait_ge(S("ssm_skip"), c + 1)
                a.activation(yu[:, c, :], yu[:, c, :], ACT.Gelu_apprx_tanh).then_inc(S("gelu"), 1)
                act.wait_ge(S("gelu"), c + 1)
                a.activation(gh[:, c, :], yu[:, c, :], ACT.Copy).then_inc(S("gelu_hi"), 1)
            half_high(0)
            for c in range(4):
                if c < 3:
                    act.wait_ge(S("glu_done"), c + 1)
                else:
                    ahead(U_GLU)
                a.activation(sig[:, c, :], bank(c), ACT.Sigmoid, bias=col(C_BGLU + c)).then_inc(S("sig"), 1)
                if c:
                    act.wait_ge(S("y_gated"), c)
                    half_square(1, c - 1)
            act.wait_ge(S("y_gated"), 4)
            half_square(1, 3)
            half_root(1)
            half_high(1)

            for j in range(4):
                ahead(U_OUT1 + j)
                residual(1, (2 * j, 2 * j + 1))

            def memory_norm():
                act.wait_ge(S("mem_loaded"), 16)
                for t in range(2):
                    a.activation(gs[:, :, :].rearrange("p a n -> p (a n)"), mtok[:, t, :], ACT.Square,
                                 accum_out=sums[:, 0, t:t + 1]).then_inc(S("mem_sq"), 1)
                    act.wait_ge(S("mem_sq"), t + 1)
                a.activation(rec[:, 0, 0:2], sums[:, 0, 0:2], ACT.Sqrt, bias=epsc[:, :], scale=1.0 / D).then_inc(S("mem_sd"), 1)
            swiglu(0, U_GU1, G_GU1, 1, memory_norm)
            for k in range(KD):
                act.wait_ge(S("mem_tr"), k + 1)
                a.activation(mh[:, k, :], bank(k, MEM), ACT.Identity, scale=col(C_MEM + k)).then_inc(S("mem_hi"), 1)
            norm(2)
            residual(3, range(4))
            ahead(U_KV)
            residual(3, range(4, 7))
            ahead(U_KV + 1)
            residual(3, range(7, 8))
            for u in range(2, 8):
                ahead(U_KV + u)

            def memory_step(l, n):
                if n in (6, 10):
                    f = (n - 6) // 4
                    act.wait_ge(S("m_pv"), MH * l + 2 * f + 2)
                    a.activation(act2[:, 8 + f, 0, :], bank(6 + f), ACT.Copy).then_inc(mix_hi, 1)
                if n % 2 == 0 and 2 <= n <= 8:
                    m = MH * l + (n - 2) // 2
                    act.wait_ge(S("m_ngm"), m + 1)
                    for i in range(4):
                        a.activation(mp[:, i, :], ps[:, 4 * BANK + MEM * i:4 * BANK + MEM * (i + 1)],
                                     ACT.Exp, bias=ngm[:, 0, i:i + 1], scale=MD ** -0.5,
                                     accum_out=sums[:, 0, i:i + 1]).then_inc(S("m_exp"), 1)
                if n % 2 and 3 <= n <= 9:
                    m = MH * l + (n - 3) // 2
                    act.wait_ge(S("m_tr"), m + 1)
                    if m:
                        act.wait_ge(S("m_pv"), m)
                    a.activation(mt[:, :, :], ps[:, 4 * BANK:6 * BANK].rearrange("p (a n) -> p a n", a=2), ACT.Copy).then_inc(S("m_pt"), 1)

            def stick(idx):
                for t in range(NH2 + 2):
                    n = NH2 * idx + t
                    z = ps[:, 3 * BANK * (t % 2):3 * BANK * (t % 2) + ZW]
                    if t < NH2:
                        act.wait_ge(S("k_z"), n + 1)
                        if t:
                            act.wait_ge(S("k_u"), 3 * n)
                        a.activation(ze[:, :], z, ACT.Abs).then_inc(S("k_e"), 1)
                        act.wait_ge(S("k_e"), 3 * n + 1)
                        a.activation(ze[:, :], ze[:, :], ACT.Exp, scale=-1.0).then_inc(S("k_e"), 1)
                        act.wait_ge(S("k_e"), 3 * n + 2)
                        a.activation(ze[:, :], ze[:, :], ACT.Ln, bias=1.0).then_inc(S("k_e"), 1)
                    if 1 <= t <= NH2:
                        act.wait_ge(S("k_cap"), 2 * n)
                        a.activation(az[(t - 1) % 2][:, :], ps[:, 3 * BANK * ((t - 1) % 2):3 * BANK * ((t - 1) % 2) + ZW], ACT.Exp).then_inc(S("k_a"), 1)
                    if t < NH2:
                        act.wait_ge(S("k_u"), 3 * (n + 1))
                        if t >= 2:
                            act.wait_ge(S("k_o"), n - 1)
                        a.activation(uh[t % 2][:, :], zu[:, :], ACT.Copy).then_inc(S("k_uh"), 1)
                    if t >= 2:
                        act.wait_ge(S("k_o"), n - 1)
                        a.activation(act2[:, t - 2, 0, :], bank(6 + t % 2), ACT.Copy).then_inc(mix_hi, 1)

            def differential():
                act.wait_ge(S("d_lamsum"), 1)
                a.activation(lam[:, 2:4], bank(3, 2), ACT.Exp).then_inc(S("d_lamexp"), 1)

                def scores_exp(hd, c):
                    m = 2 * hd + c
                    act.wait_ge(S("d_ngm"), m + 1)
                    for i in range(4):
                        z = dp[m % 4][:, ZQ[i]:ZQ[i] + wq(i)]
                        a.activation(z, z, ACT.Exp, bias=ngm[:, c, i:i + 1],
                                     accum_out=sums[:, c, i:i + 1]).then_inc(S("d_exp"), 1)

                for t in range(4 + 2):
                    if t < 4:
                        scores_exp(t, 0)
                    if t >= 2:
                        act.wait_ge(S("d_pv"), t - 1)
                        for d in range(2):
                            a.activation(osq[d][:, :], bank(6 + d), ACT.Square).then_inc(S("d_sq"), 1)
                    if 1 <= t <= 4:
                        act.wait_ge(S("d_tr"), t)
                        a.activation(dpt[:, :], ps[:, 0:ZW], ACT.Copy).then_inc(S("d_pt"), 1)
                    if t >= 2:
                        act.wait_ge(S("d_ssum"), t - 1)
                        a.activation(ors[:, :], bank(3), ACT.Sqrt, bias=hepsc[:, :], scale=1.0 / 256).then_inc(S("d_sd"), 1)
                    if t < 4:
                        scores_exp(t, 1)
                    if t >= 2:
                        for d in range(2):
                            m = 2 * (t - 2) + d
                            act.wait_ge(S("d_on"), m + 1)
                            a.activation(act2[:, m, 0, :], us[:, d, :], ACT.Copy).then_inc(mix_hi, 1)

            def conv_step(n):
                if n in (4, 7, 10, 13):
                    for t in (2 * ((n - 4) // 3), 2 * ((n - 4) // 3) + 1):
                        act.wait_ge(S("c_y"), t + 1)
                        a.activation(act2[:, t, 0, :], cy[t % 2][:, :], ACT.Copy).then_inc(mix_hi, 1)

            for l in range(NL):
                u0 = u_layer(l)
                norm(3 + 2 * l)
                for n in range(L_O):
                    ahead(u0 + n)
                    if n == 0 and l in (0, 3):
                        a.preload_act_table_set("natural_log_exp_and_others")
                    memory_step(l, n)
                    if l == 2:
                        conv_step(n)
                if l in (0, 3):
                    stick(l // 3)
                elif l == 1:
                    differential()
                else:
                    conv_step(L_O)
                for p in range(4):
                    for j in range(2):
                        ahead(u0 + L_O, p, 2, j)
                    residual(4 + 2 * l, (2 * p, 2 * p + 1))
                swiglu(1 + l, u0 + L_GU, g_gu(l), 4 + 2 * l)
            norm(11)
            for t in range(TT):
                for d in range(2):
                    n = 2 * t + d
                    act.wait_ge(S("out_tr"), n + 1)
                    a.activation(otok[:, t, 512 * d:512 * d + 512], bank(n % 4), ACT.Copy).then_inc(S("out_tile"), 1)

        @block.vector
        def _(dve):
            v = nc.vector
            chain = [0]

            def link(ins):
                chain[0] += 1
                ins.then_inc(S("vec_chain"), 1)
                dve.wait_ge(S("vec_chain"), chain[0])

            def residual(r, wait, src, mode, before={}):
                def finish(t):
                    if has_h(r):
                        hn = KD * h_index(r) + t
                        dve.wait_ge(h_hi, hn + 1)
                        v.scalar_tensor_tensor(out=hl[:, t, :], in0=x[:, t, :], scalar=col(gain_col(r) + t),
                                               in1=hh[:, t, :].bitcast(F32), op0=ALU.mult,
                                               op1=ALU.subtract).then_inc(h_ready, 1)

                def add_square(t):
                    n = KD * r + t
                    dve.wait_ge(sq_ready, n + 1)
                    if t == 0:
                        v.tensor_copy(sqacc[:, :], sqb[:, n % 2, :]).then_inc(sq_summed, 1)
                    else:
                        dve.wait_ge(sq_summed, n)
                        v.tensor_tensor(sqacc[:, :], sqacc[:, :], sqb[:, n % 2, :], ALU.add).then_inc(sq_summed, 1)
                for t in range(KD):
                    if t in before:
                        before[t]()
                    wait(t)
                    if mode == "copy":
                        ins = v.tensor_copy(x[:, t, :], src(t))
                    elif mode == "add":
                        ins = v.tensor_tensor(x[:, t, :], x[:, t, :], src(t), ALU.add)
                    else:
                        ins = v.scalar_tensor_tensor(out=x[:, t, :], in0=x[:, t, :], scalar=col(C_FIN1 + t),
                                                     in1=rstd[:, :], op0=ALU.mult, op1=ALU.mult)
                    ins.then_inc(x_new, 1)
                    if t:
                        finish(t - 1)
                        if t < KD - 1:
                            add_square(t - 1)
                finish(KD - 1)
                add_square(KD - 2)
                add_square(KD - 1)

            def norm(r, b=6):
                dve.wait_ge(sd_ready, r + 1)
                v.reciprocal(rstdc[:, :], sd[:, :]).then_inc(rstd_ready, 1)
                dve.wait_ge(rstd_ready, 3 * r + 1)
                v.tensor_tensor(sqacc[:, :].rearrange("p (t n) -> p t n", t=TT), bc(ident[:, :], TT),
                                bcl(rstdc[:, :], P), ALU.mult).then_inc(rstd_ready, 1)
                dve.wait_ge(S("rstd_row"), r + 1)
                v.tensor_copy(rstd[:, :], bank(b)).then_inc(rstd_ready, 1)

            def swiglu(s, u0, gc, r):
                def turn(i):
                    def cnt(k, c):
                        return c + k * i if isinstance(i, int) else i * k + c
                    if isinstance(i, int) and i == 0:
                        norm(r, 0)
                        dve.wait_ge(rstd_ready, 3 * (r + 1))
                    dve.wait_ge(unit_used, cnt(2, u0 + 1))
                    v.tensor_tensor(gs[:, :, :], ps[:, 4 * BANK:6 * BANK].rearrange("p (a n) -> p a n", a=2),
                                    bc(rstd[:, :], 2), ALU.mult).then_inc(acc_free, 1)
                    if not isinstance(i, int) or i + s > 0:
                        dve.wait_ge(act_ready, cnt(1, 11 * s))
                    dve.wait_ge(unit_used, cnt(2, u0 + 2))
                    v.tensor_tensor(us[:, :, :], ps[:, 6 * BANK:8 * BANK].rearrange("p (a n) -> p a n", a=2),
                                    bc(rstd[:, :], 2), ALU.mult).then_inc(acc_free, 1)
                    dve.wait_ge(silu_done, cnt(1, 11 * s + 1))
                    dve.wait_ge(acc_free, cnt(2, gc + 2))
                    v.tensor_tensor(us[:, :, :], us[:, :, :], gs[:, :, :], ALU.mult).then_inc(act_step, 1)
                    at_ = 2 * i if isinstance(i, int) else i * 2
                    dve.wait_ge(act_step, cnt(2, 22 * s + 1))
                    v.tensor_scalar(act2[:, bass.ds(at_, 2), 0, :], us[:, :, :], 1.0, None, ALU.mult).then_inc(act_step, 1)
                    dve.wait_ge(act_step, cnt(2, 22 * s + 2))
                    v.tensor_tensor(act2[:, bass.ds(at_, 2), 1, :], us[:, :, :],
                                    act2[:, bass.ds(at_, 2), 0, :].bitcast(F32), ALU.subtract).then_inc(act_ready, 1)
                loop(dve, FF // 256, turn)

            def down_tile(u0, before, t):
                if t % 4 == 3:
                    dve.wait_ge(unit_used, u0 + 6 * (t // 4) + 6)
                else:
                    dve.wait_ge(resid_done, before + 3 * (t // 4) + t % 4 + 1)

            dve.wait_ge(const_ready, 5)
            v.tensor_copy(negtri[:, :], cst[:, :]).then_inc(S("const_r"), 1)
            v.memset(sqacc[:, 0:P], -1.0).then_inc(S("const_r"), 1)
            dve.wait_ge(S("const_r"), 2)
            v.tensor_copy(negones[:, :], sqacc[:, 0:P]).then_inc(S("const_r"), 1)
            dve.wait_ge(S("ssm_loaded"), 48)
            for gi in range(2):
                ins = v.tensor_copy(rows_s[0:ST, 2, NS * gi:NS * gi + NS], ldt[0:ST, gi:gi + 1].broadcast_to([ST, NS]))
            ins.then_inc(S("rows_s_ready"), 1)
            dve.wait_ge(S("ssp_tr"), 1)
            v.tensor_copy(ssp[:, :, :], bank(1, 48).rearrange("p (r i) -> p r i", r=3)).then_inc(S("ssp_ready"), 1)
            pr = lambda k: prep[:, k, :]
            dve.wait_ge(S("dt_ready"), 1)
            v.tensor_tensor(pr(0), ssp[:, 0, :], ssp[:, 2, :], ALU.mult).then_inc(S("a_ready"), 1)
            link(v.tensor_tensor(pr(1), ssp[:, 1, :], ssp[:, 2, :], ALU.mult))
            RND = 1.5 * 2.0 ** 23
            link(v.tensor_scalar(pr(2), pr(1), 1.0 / (2 * math.pi), RND, ALU.mult, ALU.add))
            link(v.tensor_scalar(pr(2), pr(2), RND, None, ALU.subtract))
            c1, c2 = 6.28125, 0.00193500518798828125
            c3 = 2 * math.pi - c1 - c2
            for c in (c1, c2, c3):
                link(v.scalar_tensor_tensor(out=pr(1), in0=pr(2), scalar=-c, in1=pr(1), op0=ALU.mult, op1=ALU.add))
            link(v.tensor_scalar(pr(3), pr(1), 0.125, None, ALU.mult))
            link(v.tensor_tensor(pr(4), pr(3), pr(3), ALU.mult))
            link(v.tensor_scalar(pr(5), pr(4), 1 / 362880.0, -1 / 5040.0, ALU.mult, ALU.add))
            for c in (1 / 120.0, -1 / 6.0, 1.0):
                link(v.tensor_tensor(pr(5), pr(5), pr(4), ALU.mult))
                link(v.tensor_scalar(pr(5), pr(5), c, None, ALU.add))
            link(v.tensor_tensor(pr(5), pr(5), pr(3), ALU.mult))
            link(v.tensor_scalar(pr(6), pr(4), -1 / 40320.0, 1 / 720.0, ALU.mult, ALU.add))
            for c in (-1 / 24.0, 0.5):
                link(v.tensor_tensor(pr(6), pr(6), pr(4), ALU.mult))
                link(v.tensor_scalar(pr(6), pr(6), c, None, ALU.add))
            link(v.tensor_tensor(pr(6), pr(6), pr(4), ALU.mult))
            for _ in range(3):
                link(v.tensor_tensor(pr(7), pr(5), pr(6), ALU.mult))
                link(v.tensor_tensor(pr(8), pr(5), pr(5), ALU.mult))
                link(v.tensor_tensor(pr(7), pr(5), pr(7), ALU.subtract))
                link(v.tensor_scalar(pr(5), pr(7), 2.0, None, ALU.mult))
                link(v.tensor_scalar(pr(6), pr(8), 2.0, None, ALU.mult))
            link(v.tensor_scalar(pr(7), pr(6), -1.0, 1.0, ALU.mult, ALU.add))
            dve.wait_ge(S("gain_tr"), 1)
            v.tensor_copy(col(C_MIX1, 8), bank(0, 8)).then_inc(S("gain_ready"), 1)
            dve.wait_ge(S("gain_ready"), 1)
            residual(0, lambda t: dve.wait_ge(S("x_tr"), t + 1), lambda t: bank(4 + t % 4), "copy")

            link(v.memset(er[:, :, 0:1], 1.0))
            link(v.memset(ei[:, :, 0:1], 0.0))
            link(v.tensor_copy(pr(16), pr(7)))
            link(v.tensor_copy(pr(17), pr(5)))

            def double(n, i0, k):
                tiles = slice(i0, i0 + k)
                c, s = (bcl(pr(j)[:, tiles], n) for j in (16, 17))
                lo_r, lo_i = er[:, tiles, 0:n], ei[:, tiles, 0:n]
                hi_r, hi_i = er[:, tiles, n:2 * n], ei[:, tiles, n:2 * n]
                s1, s2 = (sqb[:, j, 0:k * n].rearrange("p (i n) -> p i n", i=k) for j in range(2))
                v.tensor_tensor(s1, lo_i, s, ALU.mult)
                v.tensor_tensor(s2, lo_r, s, ALU.mult)
                v.tensor_tensor(hi_r, lo_r, c, ALU.mult)
                link(v.tensor_tensor(hi_i, lo_i, c, ALU.mult))
                v.tensor_tensor(hi_r, hi_r, s1, ALU.subtract)
                link(v.tensor_tensor(hi_i, hi_i, s2, ALU.add))
                if i0 + k == ST and n < 256:
                    link(v.tensor_tensor(pr(18), pr(16), pr(16), ALU.mult))
                    link(v.tensor_tensor(pr(19), pr(17), pr(17), ALU.mult))
                    link(v.tensor_tensor(pr(17), pr(16), pr(17), ALU.mult))
                    link(v.tensor_scalar(pr(17), pr(17), 2.0, None, ALU.mult))
                    link(v.tensor_tensor(pr(16), pr(18), pr(19), ALU.subtract))
                    if n == 128:
                        v.tensor_scalar(pr(18), pr(16), 1.0, None, ALU.mult).then_inc(S("table_half"), 1)

            dve.wait_ge(S("small_loaded"), 16 * n_small[0])
            v.tensor_copy(ext[0:NH1, 0:383], ext[0:NH1, 383:384].broadcast_to([NH1, 383])).then_inc(S("rows_ready"), 1)

            norm(0)
            dve.wait_ge(rstd_ready, 3)

            def out_pair(g, dst, scale=1.0):
                src = ps[:, 2 * BANK * (g % 2):2 * BANK * (g % 2) + 2 * BANK].rearrange("p (a n) -> p a n", a=2)
                v.scalar_tensor_tensor(out=dst, in0=src, scalar=scale, in1=bc(rstd[:, :], 2),
                                       op0=ALU.mult, op1=ALU.mult).then_inc(acc_free, 1)

            def out_tokens(par, dst):
                src = ps[:, 2 * BANK * par:2 * BANK * par + 2 * BANK].rearrange("p (t n) -> p t n", t=TT)
                v.tensor_tensor(dst, src, bcl(rstdc[:, :], 256), ALU.mult).then_inc(acc_free, 1)

            def input_matrix():
                dve.wait_ge(S("rmod_ready"), 1)
                link(v.tensor_tensor(pr(9), rmod[:, :], pr(7), ALU.mult))
                link(v.tensor_scalar(pr(9), pr(9), -1.0, None, ALU.add))
                link(v.tensor_tensor(pr(10), rmod[:, :], pr(5), ALU.mult))
                link(v.tensor_tensor(pr(11), ssp[:, 0, :], ssp[:, 0, :], ALU.mult))
                link(v.tensor_tensor(pr(12), ssp[:, 1, :], ssp[:, 1, :], ALU.mult))
                link(v.tensor_tensor(pr(11), pr(11), pr(12), ALU.add))
                link(v.reciprocal(pr(11), pr(11)))
                link(v.tensor_tensor(pr(12), pr(9), ssp[:, 0, :], ALU.mult))
                link(v.tensor_tensor(pr(13), pr(10), ssp[:, 1, :], ALU.mult))
                link(v.tensor_tensor(pr(12), pr(12), pr(13), ALU.add))
                link(v.tensor_tensor(pr(12), pr(12), pr(11), ALU.mult))
                link(v.tensor_tensor(pr(13), pr(10), ssp[:, 0, :], ALU.mult))
                link(v.tensor_tensor(pr(14), pr(9), ssp[:, 1, :], ALU.mult))
                link(v.tensor_tensor(pr(13), pr(13), pr(14), ALU.subtract))
                link(v.tensor_tensor(pr(13), pr(13), pr(11), ALU.mult))
                t1 = sqb[:, 0, 0:ST * HG].rearrange("p (i h) -> p i h", h=HG)
                t2 = sqb[:, 1, 0:ST * HG].rearrange("p (i h) -> p i h", h=HG)
                for r in range(2):
                    link(v.tensor_tensor(t1, braw[:, r, :, :], bcl(pr(12), HG), ALU.mult))
                    link(v.tensor_tensor(t2, braw[:, 1 - r, :, :], bcl(pr(13), HG), ALU.mult))
                    for gi in range(2):
                        rows = slice(NS * gi, NS * gi + NS)
                        v.tensor_tensor(bpre[rows, r, :, HG * gi:HG * gi + HG], t1[rows], t2[rows],
                                        ALU.add if r else ALU.subtract).then_inc(S("bpre_ready"), 1)
                    dve.wait_ge(S("bpre_ready"), 2 * (r + 1))

            def small_vectors():
                dve.wait_ge(S("small_tr"), 1)
                link(v.tensor_copy(cols[:, 8:C_END], bank(4, C_END - 8, 8)))
                link(v.tensor_copy(cols[:, C_CONV:C_CONV + 24], bank(4, 24, P)))
                v.tensor_scalar(gdiff[:, :], col(C_DIFF, 2), 1.0 - LAMBDA_INIT, None, ALU.mult).then_inc(S("cols_ready"), 1)

                dve.wait_ge(const_ready, 5)
                for r in range(2):
                    for c in range(4):
                        src = ps[:, (5 + r) * BANK + P * c:(5 + r) * BANK + P * c + P].rearrange("p (j g h) -> p j g h", j=4, g=2)
                        for gi in range(2):
                            rows = slice(NS * gi, NS * gi + NS)
                            v.tensor_scalar(ct[rows, 4 * c:4 * c + 4, r, HG * gi:HG * gi + HG], src[rows, :, gi, :],
                                            -1.0 if r else 1.0, None, ALU.mult).then_inc(S("ct_ready"), 1)

            def table_steps(u):
                if u == 2:
                    for e in range(6):
                        double(1 << e, 0, ST)
                    for i0 in (0, ST // 2):
                        double(64, i0, ST // 2)
                if u in (3, 4):
                    for i0 in (8 * (u - 3), 8 * (u - 3) + 4):
                        double(128, i0, 4)

            for u in range(8):
                if u == 0:
                    input_matrix()
                if u == 3:
                    small_vectors()
                table_steps(u)
                if u == 5:
                    dve.wait_ge(S("bt_tr"), 1)
                    dve.wait_ge(S("ext_stored"), 16)
                    for r in range(2):
                        v.tensor_copy(bt[:, :, r, :], bank(4 + r).rearrange("p (c n) -> p c n", c=4)).then_inc(S("bt_ready"), 1)
                dve.wait_ge(unit_used, u + 1)
                if u < 6:
                    out_pair(u, (yu, q1, k1)[u // 2][:, 2 * (u % 2):2 * (u % 2) + 2, :])
                else:
                    out_tokens(u % 2, v1[:, :, 256 * (u % 2):256 * (u % 2) + 256])

            for b in bsb:
                v.memset(b[0:64, 448:512], NEG).then_inc(S("a1_corner"), 1)

            for t in range(NH1 + 2):
                if 1 <= t <= NH1:
                    h = t - 1
                    dve.wait_ge(S("a1_exp"), 4 * t)
                    link(v.reciprocal(rec[:, h % 2, :], sums[:, h % 2, :]))
                    for i in range(4):
                        z = pbuf[h % 2][:, ZQ[i]:ZQ[i] + wq(i)]
                        v.tensor_scalar(z, z, rec[:, h % 2, i:i + 1], None, ALU.mult).then_inc(S("a1_p"), 1)
                if t < NH1:
                    h = t
                    dve.wait_ge(S("a1_z"), h + 1)
                    dve.wait_ge(S("a1_bcopy"), 2 * h + 2)
                    dve.wait_ge(S("a1_corner"), 2)
                    if h >= 2:
                        dve.wait_ge(S("a1_tr"), h - 1)
                    for i in range(4):
                        v.scalar_tensor_tensor(out=pbuf[h % 2][:, ZQ[i]:ZQ[i] + wq(i)],
                                               in0=ps[:, ZQ[i]:ZQ[i] + wq(i)], scalar=DH1 ** -0.5,
                                               in1=bsb[h % 2][:, T - wq(i):T], op0=ALU.mult, op1=ALU.add).then_inc(S("a1_s"), 1)
                    for i in range(4):
                        dve.wait_ge(S("a1_s"), 4 * h + i + 1)
                        v.tensor_reduce(mx[:, h % 2, i:i + 1], pbuf[h % 2][:, ZQ[i]:ZQ[i] + wq(i)], AX.X, ALU.max).then_inc(S("a1_mx"), 1)
                    dve.wait_ge(S("a1_mx"), 4 * (h + 1))
                    v.tensor_scalar(ngm[:, h % 2, :], mx[:, h % 2, :], -1.0, None, ALU.mult).then_inc(S("a1_ngm"), 1)
                if t >= 2 and t % 2 == 1:
                    f = (t - 2) // 2
                    dve.wait_ge(S("a1_pv"), 2 * f + 2)
                    v.tensor_copy(ya[:, f, :], bank(6)).then_inc(S("ya_ready"), 1)

            def half_sum(n, c):
                m = 4 * n + c
                dve.wait_ge(S("hn_sq"), m + 1)
                if c == 0:
                    v.tensor_copy(sqacc[:, :], sqb[:, m % 2, :]).then_inc(S("hn_sum"), 1)
                else:
                    dve.wait_ge(S("hn_sum"), m)
                    v.tensor_tensor(sqacc[:, :], sqacc[:, :], sqb[:, m % 2, :], ALU.add).then_inc(S("hn_sum"), 1)

            def half_low(n, src, g, slot0):
                dve.wait_ge(S("hn_sd"), n + 1)
                link(v.reciprocal(rstd[:, :], rstd[:, :]))
                for c in range(4):
                    v.scalar_tensor_tensor(out=src[:, c, :], in0=src[:, c, :], scalar=col(g + c), in1=rstd[:, :],
                                           op0=ALU.mult, op1=ALU.mult).then_inc(S("hn_y"), 1)
                for c in range(4):
                    m = 4 * n + c
                    dve.wait_ge(mix_hi, m + 1)
                    v.tensor_tensor(act2[:, slot0 + c, 1, :], src[:, c, :], act2[:, slot0 + c, 0, :].bitcast(F32),
                                    ALU.subtract).then_inc(mix_ready, 1)

            for c in range(4):
                half_sum(0, c)

            def back(i):
                dve.wait_ge(S("ssm_x"), 2 * i + 2)
                if i:
                    dve.wait_ge(S("ssm_n"), 4 * i)
                for c in range(2):
                    v.tensor_tensor_scan(out=ss[c][:, :], data0=rmod[:, i:i + 1].broadcast_to([P, T]), data1=sx[c][:, :],
                                         initial=0.0, op0=ALU.mult, op1=ALU.add).then_inc(S("ssm_scan"), 1)
                dve.wait_ge(S("ssm_scan"), 2 * i + 2)
                if i:
                    dve.wait_ge(S("ssm_y"), 2 * i)
                for n, (c, e) in enumerate(((0, er), (1, ei), (0, ei), (1, er))):
                    v.tensor_tensor(sn[n][:, :], ss[c][:, :], e[:, i, :], ALU.mult).then_inc(S("ssm_n"), 1)

            for i in range(ST + 1):
                if i < ST:
                    dve.wait_ge(S("ssm_bu"), i + 1)
                    dve.wait_ge(S("table_high"), 6 * (i // 2 + 1))
                    if i:
                        dve.wait_ge(S("ssm_x"), 2 * i)
                    for n, (c, e) in enumerate(((0, er), (1, ei), (1, er), (0, ei))):
                        v.tensor_tensor(sm[n][:, :], bank(2 * (i % 2) + c), e[:, i, :], ALU.mult).then_inc(S("ssm_m"), 1)
                if i:
                    back(i - 1)
            for c in range(4):
                dve.wait_ge(S("ssm_yd"), 4 * c + 4)
                v.scalar_tensor_tensor(out=yu[:, c, :], in0=yu[:, c, :], scalar=col(C_D + c), in1=bank(4 + c),
                                       op0=ALU.mult, op1=ALU.add).then_inc(S("ssm_skip"), 1)
            for c in range(4):
                dve.wait_ge(S("gelu_hi"), c + 1)
                v.tensor_tensor(gl[:, c, :], yu[:, c, :], gh[:, c, :].bitcast(F32), ALU.subtract).then_inc(S("gelu_lo"), 1)

            half_low(0, ya, C_ATT, 4)
            for c in range(4):
                dve.wait_ge(S("sig"), c + 1)
                v.tensor_tensor(yu[:, c, :], yu[:, c, :], sig[:, c, :], ALU.mult).then_inc(S("y_gated"), 1)
                if c:
                    half_sum(1, c - 1)
            half_sum(1, 3)
            half_low(1, yu, C_SSM, 0)

            residual(1, lambda t: dve.wait_ge(unit_used, U_OUT1 + t // 2 + 1) if t % 2 else dve.wait_ge(resid_done, t // 2 + 1), lambda t: bank((4 + t) % 8), "add")
            swiglu(0, U_GU1, G_GU1, 1)
            dve.wait_ge(S("mem_sd"), 1)
            link(v.reciprocal(rec[:, 1, 0:2], rec[:, 0, 0:2]))
            for t in range(2):
                v.tensor_scalar(mtok[:, t, :], mtok[:, t, :], rec[:, 1, t:t + 1], None, ALU.mult).then_inc(S("mem_scaled"), 1)
            residual(2, lambda t: down_tile(U_DN1, 4, t), lambda t: bank(t), "add")
            for k in range(KD):
                dve.wait_ge(S("mem_hi"), k + 1)
                v.scalar_tensor_tensor(out=ml[:, k, :], in0=bank(k, MEM), scalar=col(C_MEM + k),
                                       in1=mh[:, k, :].bitcast(F32), op0=ALU.mult, op1=ALU.subtract).then_inc(S("mem_ready"), 1)
            norm(2)
            dve.wait_ge(rstd_ready, 9)

            def kv_out(j, i):
                dve.wait_ge(unit_used, U_KV + 2 * i + j + 1 if isinstance(i, int) else i * 2 + (U_KV + j + 1))
                src = ps[:, 2 * BANK * j:2 * BANK * j + 2 * BANK].rearrange("p (a n) -> p a n", a=2)[:, :, 0:MEM]
                dst = (km, vm)[j][:, bass.ds(i, 1), :, :].rearrange("p o a n -> p (o a) n")
                v.tensor_scalar(dst, src, 1.0, None, ALU.mult).then_inc(acc_free, 1)
            residual(3, lambda t: None, lambda t: None, "norm",
                     before={4: lambda: kv_out(0, 0), 7: lambda: kv_out(1, 0)})
            with dve.Fori(1, NL) as i:
                for j in range(2):
                    kv_out(j, i)

            def mix_low(slot, src, n):
                dve.wait_ge(mix_hi, n + 1)
                v.tensor_tensor(act2[:, slot, 1, :], src, act2[:, slot, 0, :].bitcast(F32), ALU.subtract).then_inc(mix_ready, 1)

            def memory_step(l, n):
                if n in (6, 10):
                    f = (n - 6) // 4
                    mix_low(8 + f, bank(6 + f), mix_index(l, 8 + f))
                if n % 2 == 0 and 2 <= n <= 8:
                    m = MH * l + (n - 2) // 2
                    dve.wait_ge(S("m_z"), m + 1)
                    src = ps[:, 4 * BANK:6 * BANK].rearrange("p (i n) -> p i n", i=4)
                    link(v.tensor_reduce(mx[:, 0, :], src, AX.X, ALU.max))
                    v.tensor_scalar(ngm[:, 0, :], mx[:, 0, :], -(MD ** -0.5), None, ALU.mult).then_inc(S("m_ngm"), 1)
                    dve.wait_ge(S("m_exp"), 4 * (m + 1))
                    link(v.reciprocal(rec[:, 0, :], sums[:, 0, :]))
                    v.tensor_tensor(mp[:, :, :], mp[:, :, :], bcl(rec[:, 0, :], MEM), ALU.mult).then_inc(S("m_p"), 1)

            def stick(idx, m0):
                for t in range(NH2 + 2):
                    n = NH2 * idx + t
                    if 1 <= t <= NH2:
                        z = ps[:, 3 * BANK * ((t - 1) % 2):3 * BANK * ((t - 1) % 2) + 3 * BANK]
                        dve.wait_ge(S("k_cum"), n)
                        z3 = z.rearrange("p (b n) -> p b n", b=3)[:, :, 0:P]
                        v.tensor_tensor(z3, z3, bc(cap[:, :], 3), ALU.min).then_inc(S("k_cap"), 1)
                        v.tensor_tensor(z[:, ZK[3]:ZK[3] + P], z[:, ZK[3]:ZK[3] + P], cap[:, :], ALU.min).then_inc(S("k_cap"), 1)
                    if t < NH2:
                        z = ps[:, 3 * BANK * (t % 2):3 * BANK * (t % 2) + ZW]
                        dve.wait_ge(S("k_e"), 3 * (n + 1))
                        if t:
                            dve.wait_ge(S("k_uh"), n)
                        v.scalar_tensor_tensor(out=zu[:, :], in0=z, scalar=0.0, in1=ze[:, :], op0=ALU.max,
                                               op1=ALU.add).then_inc(S("k_u"), 1)
                        dve.wait_ge(S("k_u"), 3 * n + 1)
                        u2 = zu[:, 0:1024].rearrange("p (b n) -> p b n", b=2)[:, :, 0:P]
                        v.tensor_tensor(u2, u2, bc(mask[:, :], 2), ALU.mult).then_inc(S("k_u"), 1)
                        u3 = zu[:, ZK[3]:ZK[3] + 2 * P].rearrange("p (b n) -> p b n", b=2)
                        v.tensor_tensor(u3, u3, bc(mask[:, :], 2), ALU.mult).then_inc(S("k_u"), 1)
                        dve.wait_ge(S("k_uh"), n + 1)
                        v.tensor_tensor(ul[t % 2][:, :], zu[:, :], uh[t % 2][:, :].bitcast(F32), ALU.subtract).then_inc(S("k_ul"), 1)
                    if t >= 2:
                        mix_low(t - 2, bank(6 + t % 2), m0 + 2 + t - 2)

            def differential(m0):
                for c in range(2):
                    v.tensor_tensor(lam[:, c:c + 1], col(C_LAM + 2 * c), col(C_LAM + 2 * c + 1), ALU.mult).then_inc(S("d_lam"), 1)
                dve.wait_ge(S("d_lamexp"), 1)
                link(v.tensor_tensor(lam[:, 4:5], lam[:, 3:4], lam[:, 2:3], ALU.subtract))
                link(v.tensor_scalar(lam[:, 4:5], lam[:, 4:5], -LAMBDA_INIT, None, ALU.add))
                link(v.tensor_reduce(lam[:, 5:6], mask[:, :], AX.X, ALU.add))
                link(v.tensor_scalar(lam[:, 5:6], lam[:, 5:6], -1.0, float(T), ALU.mult, ALU.add))
                link(v.tensor_tensor_scan(out=dist[:, :], data0=ones[:, 0:1].broadcast_to([P, T]),
                                          data1=cst[:, 0:1].broadcast_to([P, T]), initial=lam[:, 5:6],
                                          op0=ALU.mult, op1=ALU.add))
                link(v.tensor_scalar(dneg[:, :], dist[:, :], 0.0, NEG, ALU.is_lt, ALU.mult))

                def add_bias(hd, c):
                    m = 2 * hd + c
                    if c == 0:
                        link(v.scalar_tensor_tensor(out=dbias[:, :], in0=dist[:, :], scalar=-2.0 ** (-8.0 * (hd + 1) / 4),
                                                    in1=dneg[:, :], op0=ALU.mult, op1=ALU.add))
                    dve.wait_ge(S("d_z"), m + 1)
                    if hd >= 2:
                        dve.wait_ge(S("d_tr"), hd - 1)
                    for i in range(4):
                        v.tensor_tensor(dp[m % 4][:, ZQ[i]:ZQ[i] + wq(i)], ps[:, 3 * BANK * c + ZQ[i]:3 * BANK * c + ZQ[i] + wq(i)],
                                        dbias[:, T - wq(i):T], ALU.add).then_inc(S("d_s"), 1)

                def row_max(hd, c):
                    m = 2 * hd + c
                    for i in range(4):
                        dve.wait_ge(S("d_s"), 4 * m + i + 1)
                        v.tensor_reduce(mx[:, c, i:i + 1], dp[m % 4][:, ZQ[i]:ZQ[i] + wq(i)], AX.X, ALU.max).then_inc(S("d_mx"), 1)
                    dve.wait_ge(S("d_mx"), 4 * (m + 1))
                    v.tensor_scalar(ngm[:, c, :], mx[:, c, :], -1.0, None, ALU.mult).then_inc(S("d_ngm"), 1)

                def row_sums(hd, c):
                    dve.wait_ge(S("d_exp"), 4 * (2 * hd + c + 1))
                    link(v.reciprocal(rec[:, c, :], sums[:, c, :]))
                    if c:
                        link(v.tensor_scalar(rec[:, 1, :], rec[:, 1, :], lam[:, 4:5], None, ALU.mult))

                def combine(hd):
                    p0, p1 = dp[2 * hd % 4], dp[(2 * hd + 1) % 4]
                    for i in range(4):
                        z = p0[:, ZQ[i]:ZQ[i] + wq(i)]
                        v.tensor_scalar(z, z, rec[:, 0, i:i + 1], None, ALU.mult).then_inc(S("d_p"), 1)
                    for i in range(4):
                        z = slice(ZQ[i], ZQ[i] + wq(i))
                        dve.wait_ge(S("d_p"), 8 * hd + i + 1)
                        v.scalar_tensor_tensor(out=p0[:, z], in0=p1[:, z], scalar=rec[:, 1, i:i + 1],
                                               in1=p0[:, z], op0=ALU.mult, op1=ALU.add).then_inc(S("d_p"), 1)

                def head_norm(hd):
                    dve.wait_ge(S("d_sd"), hd + 1)
                    link(v.reciprocal(ors[:, :], ors[:, :]))
                    if hd:
                        dve.wait_ge(mix_hi, m0 + 2 + 2 * hd)
                    for d in range(2):
                        v.scalar_tensor_tensor(out=us[:, d, :], in0=bank(6 + d), scalar=gdiff[:, d:d + 1], in1=ors[:, :],
                                               op0=ALU.mult, op1=ALU.mult).then_inc(S("d_on"), 1)
                    for d in range(2):
                        mix_low(2 * hd + d, us[:, d, :], m0 + 2 + 2 * hd + d)

                for t in range(4 + 2):
                    if 1 <= t <= 4:
                        row_sums(t - 1, 0)
                        row_sums(t - 1, 1)
                    if t < 4:
                        add_bias(t, 0)
                    if 1 <= t <= 4:
                        combine(t - 1)
                    if t < 4:
                        row_max(t, 0)
                        add_bias(t, 1)
                        row_max(t, 1)
                    if t >= 2:
                        head_norm(t - 2)

            def conv_step(n):
                if n in (4, 7, 10, 13):
                    for t in (2 * ((n - 4) // 3), 2 * ((n - 4) // 3) + 1):
                        mix_low(t, cy[t % 2][:, :], mix_index(2, t))
                if n in (3, 6, 9, 12):
                    dve.wait_ge(acc_free, g_in(2) + n + 1)
                    for t in (2 * (n // 3) - 2, 2 * (n // 3) - 1):
                        if t:
                            dve.wait_ge(S("c_y"), t)
                        if t >= 2:
                            dve.wait_ge(mix_ready, mix_index(2, t - 2) + 1)
                        else:
                            link(v.memset(cv[:, 0:2], 0.0))
                        link(v.tensor_tensor(cv[:, 2:T + 2], k2[:, t, :], vf[:, t, :], ALU.mult))
                        y = cy[t % 2][:, :]
                        link(v.tensor_scalar(y, cv[:, 2:T + 2], col(C_CONV + 16 + t), None, ALU.mult))
                        link(v.scalar_tensor_tensor(out=y, in0=cv[:, 1:T + 1], scalar=col(C_CONV + 8 + t), in1=y,
                                                    op0=ALU.mult, op1=ALU.add))
                        link(v.scalar_tensor_tensor(out=y, in0=cv[:, 0:T], scalar=col(C_CONV + t), in1=y,
                                                    op0=ALU.mult, op1=ALU.add))
                        v.tensor_tensor(y, y, q2[:, t, :], ALU.mult).then_inc(S("c_y"), 1)

            for l in range(NL):
                u0 = u_layer(l)
                norm(3 + 2 * l)
                dve.wait_ge(rstd_ready, 3 * (4 + 2 * l))
                scale = 1.0 if l == 2 else DH2 ** -0.5

                m0 = 8 + 10 * l
                for n in range(L_O):
                    dve.wait_ge(unit_used, u0 + n + 1)
                    stream, p = divmod(n - 1, 4) if l != 2 else ((n - 1) % 3, (n - 1) // 3)
                    if n == 0:
                        out_pair(0, mq[:, :, :])
                    elif stream == 2 and l != 2:
                        out_tokens(n % 2, v2[:, :, 256 * p:256 * p + 256])
                    else:
                        out_pair(n % 2, (q2, k2, vf)[stream][:, 2 * p:2 * p + 2, :], 1.0 if stream else scale)
                    memory_step(l, n)
                    if l == 2:
                        conv_step(n)
                if l in (0, 3):
                    stick(l // 3, m0)
                elif l == 1:
                    differential(m0)
                else:
                    conv_step(L_O)
                r = 4 + 2 * l
                residual(r, lambda t: dve.wait_ge(unit_used, u0 + L_O + 2 * (t // 2) + 2) if t % 2 else dve.wait_ge(resid_done, 10 * (l + 1) + t // 2 + 1), lambda t: bank((4 + t) % 8), "add")
                swiglu(1 + l, u0 + L_GU, g_gu(l), r)
                residual(r + 1, lambda t: down_tile(u0 + L_DN, 10 * (l + 1) + 4, t), lambda t: bank(t), "add")
            norm(11)
            dve.wait_ge(rstd_ready, 36)
            for t in range(KD):
                v.scalar_tensor_tensor(out=x[:, t, :], in0=x[:, t, :], scalar=col(C_FIN2 + t), in1=rstd[:, :],
                                       op0=ALU.mult, op1=ALU.mult).then_inc(S("out_scaled"), 1)

        @block.tensor
        def _(pe):
            mm, tr = nc.tensor.matmul, nc.tensor.transpose

            def three(dst, wh, wl, xh, xl, first, last):
                mm(dst, wh, xh, start=first, stop=False, skip_group_check=True)
                mm(dst, wh, xl, start=False, stop=False, skip_group_check=True)
                return mm(dst, wl, xh, start=False, stop=last, skip_group_check=True)

            def unit_ready(u, i=0, per=0):
                pe.wait_ge(lo_made, u + 1 + per * i if isinstance(i, int) else i * per + (u + 1))

            def feature_tiles(slot, banks, xh, xl, kn=KD, n=2, k0=0, first=True, last=True, gate=None, outer_k=True, ks=None, opens=0, closes=None):
                ends = {}
                ks = range(kn) if ks is None else ks
                order = [(k, c) for k in ks for c in range(n)] if outer_k else [(k, c) for c in range(n) for k in ks]
                for k, c in order:
                    if gate is not None and c == 0:
                        gate(k)
                    w = slice(k * P * n + P * c, k * P * n + P * c + P)
                    ends[c] = three(banks(c), whi[:, slot, w], wlo[:, slot, w], xh(k0 + k), xl(k0 + k),
                                    first and k == opens, last and k == (kn - 1 if closes is None else closes))
                return ends

            def token_tiles(slot, par, th, tl, n=TT, step=256):
                for t in range(n):
                    dst = ps[:, 2 * BANK * par + step * t:2 * BANK * par + step * t + 256]
                    for k in range(KD):
                        hs, ls = th[:, k, P * t:P * t + P], tl[:, k, P * t:P * t + P]
                        w = slice(256 * k, 256 * k + 256)
                        mm(dst, hs, whi[:, slot, w], start=k == 0, stop=False, skip_group_check=True)
                        mm(dst, ls, whi[:, slot, w], start=False, stop=False, skip_group_check=True)
                        e = mm(dst, hs, wlo[:, slot, w], start=False, stop=k == KD - 1, skip_group_check=True)
                return e

            XH, XL = (lambda k: hh[:, k, :]), (lambda k: hl[:, k, :])
            AH, AL = (lambda k: act2[:, k, 0, :]), (lambda k: act2[:, k, 1, :])

            def norm_sum(r, b=6):
                pe.wait_ge(sq_summed, KD * (r + 1))
                for t in range(TT):
                    e = mm(bank(b + 1, 1, t), sqacc[:, P * t:P * t + P], ones[:, 0:1], start=True, stop=True)
                e.then_inc(ssum_done, 1)

            def norm_row(r, b=6):
                pe.wait_ge(rstd_ready, 3 * r + 2)
                mm(bank(b), ones[:, :], sqacc[:, :], start=True, stop=True).then_inc(S("rstd_row"), 1)

            def first_turn(r, u0, b, nb):
                gate = lambda k: pe.wait_ge(h_ready, KD * h_index(r) + k + 1)
                pe.wait_ge(x_new, KD * r + 4)
                unit_ready(u0)
                feature_tiles(u0 % 2, lambda c: bank(b + c), XH, XL, gate=gate)[1].then_inc(unit_used, 1)
                norm_sum(r, nb)
                unit_ready(u0 + 1)
                for ks in (range(4), range(4, KD)):
                    e = feature_tiles((u0 + 1) % 2, lambda c: bank(b + 2 + c), XH, XL, ks=ks)[1]
                    if ks[0] == 0:
                        norm_row(r, nb)
                e.then_inc(unit_used, 1)

            pe.wait_ge(const_ready, 5)
            pe.wait_ge(S("rows_s_ready"), 1)
            for r in range(3):
                e = tr(bank(1, ST, ST * r), rows_s[0:ST, r, :], ident[0:ST, 0:ST])
            e.then_inc(S("ssp_tr"), 1)
            pe.wait_ge(S("gain_loaded"), 16)
            tr(bank(0, 8), rows_a[C_MIX1:C_MIX1 + 8, :], ident[0:8, 0:8]).then_inc(S("gain_tr"), 1)
            pe.wait_ge(S("x_loaded"), 16)

            def x_tile(f):
                for t in range(TT):
                    e = tr(bank(4 + f % 4, P, P * t), xtok[:, t, P * f:P * f + P], ident[:, :])
                e.then_inc(S("x_tr"), 1)
            for f in range(KD):
                if f >= 4:
                    pe.wait_ge(x_new, f - 3)
                x_tile(f)
            first_turn(0, 0, 0, 6)
            for u in range(2, 8):
                unit_ready(u)
                pe.wait_ge(acc_free, u - 1)
                if u < 6:
                    e = feature_tiles(u % 2, lambda c: bank(2 * (u % 2) + c), XH, XL)[1]
                else:
                    e = token_tiles(u % 2, u % 2, hh, hl)
                e.then_inc(unit_used, 1)
                if u == 2:
                    pe.wait_ge(S("rows_ready"), 1)
                    pe.wait_ge(rstd_ready, 3)
                    tr(bank(4, C_END), rows_a[0:C_END, :], ident[0:C_END, 0:C_END])
                    tr(bank(4, 24, P), rows_b[0:24, :], ident[0:24, 0:24])
                    for r in range(2):
                        for c in range(4):
                            e = tr(bank(5 + r, P, P * c), craw[:, r, c, :, :].rearrange("p d s -> p (d s)"), ident[:, :])
                    e.then_inc(S("small_tr"), 1)
                if u == 4:
                    pe.wait_ge(S("bpre_ready"), 4)
                    pe.wait_ge(S("ct_ready"), 16)
                    for r in range(2):
                        for c in range(4):
                            e = tr(bank(4 + r, P, P * c), bpre[:, r, 4 * c:4 * c + 4, :].rearrange("p i h -> p (i h)"), ident[:, :])
                    e.then_inc(S("bt_tr"), 1)
            pe.wait_ge(acc_free, 8)
            pe.wait_ge(rstd_ready, 3)
            for t in range(NH1 + 2):
                if t < NH1:
                    h, f, rows = t, t // 2, slice(64 * (t % 2), 64 * (t % 2) + 64)
                    pe.wait_ge(S(f"hankel{h % 2}"), 16 * (h // 2 + 1))
                    if h:
                        pe.wait_ge(S("a1_bcopy"), 2 * h)
                    mm(bank(7), flip[:, :], hankel_tile(h)[:, :], start=True, stop=True).then_inc(S("a1_bias"), 1)
                    if h:
                        pe.wait_ge(S("a1_s"), 4 * h)
                    for i in (0, 2, 3, 1):
                        e = mm(ps[:, ZQ[i]:ZQ[i] + wq(i)], q1[rows, f, P * i:P * i + P], k1[rows, f, 0:wq(i)],
                               start=i != 2, stop=True, skip_group_check=True)
                    e.then_inc(S("a1_z"), 1)
                if 1 <= t <= NH1:
                    h = t - 1
                    pe.wait_ge(S("a1_p"), 4 * t)
                    if h:
                        pe.wait_ge(S("a1_pt"), h)
                    for j in (0, 1, 3, 2):
                        for i in range(j, 4):
                            o = 3 * BANK + ZK[j] + P * (i - j)
                            e = tr(ps[:, o:o + P], pbuf[h % 2][:, ZQ[i] + P * j:ZQ[i] + P * j + P], ident[:, :])
                    e.then_inc(S("a1_tr"), 1)
                if t >= 2:
                    h = t - 2
                    f, r0 = h // 2, 64 * (h % 2)
                    pe.wait_ge(S("a1_pt"), h + 1)
                    if h >= 2:
                        pe.wait_ge(S("ya_ready"), f)
                    for j in range(4):
                        e = mm(ps[r0:r0 + 64, 6 * BANK + P * j:7 * BANK], v1[:, j, DH1 * h:DH1 * h + DH1],
                               ptb[h % 2][:, ZK[j]:ZK[j] + wk(j)], start=j == 0, stop=j == 3, skip_group_check=True)
                    e.then_inc(S("a1_pv"), 1)
            def y_out(i):
                pe.wait_ge(S("ssm_y"), 2 * i + 2)
                c, j = i // 4, i % 4
                dst = ps[32 * j:32 * j + 32, (4 + c) * BANK:(5 + c) * BANK]
                mm(dst, ct[:, i, 0, :], sy[0][:, :], start=True, stop=False, skip_group_check=True)
                mm(dst, ct[:, i, 1, :], sy[1][:, :], start=False, stop=True, skip_group_check=True).then_inc(S("ssm_yd"), 1)
            def half_ssum(n):
                pe.wait_ge(S("hn_sum"), 4 * (n + 1))
                mm(bank(6), ones[:, :], sqacc[:, :], start=True, stop=True).then_inc(S("hn_ssum"), 1)
            pe.wait_ge(S("ya_ready"), 4)
            for i in range(ST + 2):
                if i < ST:
                    c, rows = i // 4, slice(32 * (i % 4), 32 * (i % 4) + 32)
                    if i >= 2:
                        pe.wait_ge(S("ssm_m"), 4 * (i - 1))
                    for r in range(2):
                        e = mm(bank(2 * (i % 2) + r), bt[rows, c, r, :], yu[rows, c, :], start=True, stop=True)
                    e.then_inc(S("ssm_bu"), 1)
                if i == 1:
                    half_ssum(0)
                if i >= 2:
                    if i == 2:
                        pe.wait_ge(S("hn_sd"), 1)
                    y_out(i - 2)
            unit_ready(U_GLU)
            pe.wait_ge(S("gelu_lo"), 4)
            for c in range(4):
                for k in range(4):
                    w = slice(512 * k + P * c, 512 * k + P * c + P)
                    e = three(bank(c), whi[:, 0, w], wlo[:, 0, w], gh[:, k, :], gl[:, k, :], k == 0, k == 3)
                e.then_inc(S("glu_done") if c < 3 else unit_used, 1)
            half_ssum(1)
            for p in range(4):
                unit_ready(U_OUT1 + p)
                slot, banks = (U_OUT1 + p) % 2, lambda c: bank((4 + 2 * p + c) % 8)
                if p == 0:
                    pe.wait_ge(mix_ready, 4)
                    feature_tiles(slot, banks, AH, AL, ks=range(4, KD), last=False, opens=4)
                    pe.wait_ge(mix_ready, 8)
                    ends = feature_tiles(slot, banks, AH, AL, ks=range(4), first=False, closes=3, outer_k=False)
                else:
                    ends = feature_tiles(slot, banks, AH, AL, outer_k=False)
                ends[0].then_inc(resid_done, 1)
                ends[1].then_inc(unit_used, 1)

            def swiglu(s, u0, gc, r):
                first_turn(r, u0, 4, 0)
                with pe.Fori(1, FF // 256) as i:
                    for j in range(2):
                        unit_ready(u0 + j, i, 2)
                        pe.wait_ge(acc_free, i * 2 + (gc + j - 1))
                        feature_tiles((u0 + j) % 2, lambda c: bank(4 + 2 * j + c), XH, XL)[1].then_inc(unit_used, 1)

                def down(i):
                    for j in range(6):
                        slot = (u0 + 22 + j) % 2
                        unit_ready(u0 + 22 + j, i, 6)
                        pe.wait_ge(act_ready, 11 * s + min(2 * j + 2, 11))
                        kn = min(4, KF - 4 * j)
                        base = 2048 * i if isinstance(i, int) else i * 2048
                        ends = feature_tiles(slot, lambda c: ps[:, bass.ds(base + 512 * c, 512)], AH, AL, kn=kn, n=4,
                                             k0=4 * j, first=j == 0, last=j == 5, outer_k=j < 5)
                        if j == 5:
                            for c in range(3):
                                ends[c].then_inc(resid_done, 1)
                        ends[3].then_inc(unit_used, 1)
                pe.wait_ge(rstd_ready, 3 * (r + 1))
                loop(pe, 2, down, peel=0)

            swiglu(0, U_GU1, G_GU1, 1)
            pe.wait_ge(S("mem_scaled"), 2)
            for k in range(KD):
                pe.wait_ge(x_new, 2 * KD + k + 1)
                for t in range(2):
                    e = tr(bank(k, P, P * t), mtok[:, t, P * k:P * k + P], ident[:, :])
                e.then_inc(S("mem_tr"), 1)
            pe.wait_ge(S("mem_ready"), KD)
            norm_sum(2)

            def kv(i):
                for j in range(2):
                    if isinstance(i, int) and i == 0 and j == 1:
                        norm_row(2)
                    unit_ready(U_KV + j, i, 2)
                    if not (isinstance(i, int) and i == 0):
                        pe.wait_ge(acc_free, G_KV + 2 * i + j - 1 if isinstance(i, int) else i * 2 + (G_KV + j - 1))
                    slot = (U_KV + j) % 2
                    if j == 0:
                        e = feature_tiles(slot, lambda c: bank(c, MEM), lambda k: mh[:, k, :], lambda k: ml[:, k, :])[1]
                    else:
                        e = token_tiles(slot, 1, mh, ml, n=2, step=BANK)
                    e.then_inc(unit_used, 1)
            loop(pe, NL, kv, peel=1)
            pe.wait_ge(acc_free, G_L0)

            def memory_step(l, n):
                if n % 2 == 0 and 4 <= n <= 10:
                    h = (n - 4) // 2
                    f, r0 = h // 2, 64 * (h % 2)
                    pe.wait_ge(S("m_pt"), MH * l + h + 1)
                    for j in range(2):
                        e = mm(ps[r0:r0 + 64, (6 + f) * BANK:(7 + f) * BANK], vm[:, l, j, MD * h:MD * h + MD],
                               mt[:, j, :], start=j == 0, stop=j == 1, skip_group_check=True)
                    e.then_inc(S("m_pv"), 1)
                if n % 2 == 0 and 2 <= n <= 8:
                    h = (n - 2) // 2
                    f, rows = h // 2, slice(64 * (h % 2), 64 * (h % 2) + 64)
                    for i in range(4):
                        o = 4 * BANK + MEM * i
                        e = mm(ps[:, o:o + MEM], mq[rows, f, P * i:P * i + P], km[rows, l, f, :], start=i % 2 == 0,
                               stop=True, skip_group_check=True)
                    e.then_inc(S("m_z"), 1)
                if n % 2 and 3 <= n <= 9:
                    h = (n - 3) // 2
                    pe.wait_ge(S("m_p"), MH * l + h + 1)
                    for j in range(2):
                        for i in range(4):
                            e = tr(bank(4 + j, P, P * i), mp[:, i, P * j:P * j + P], ident[:, :])
                    e.then_inc(S("m_tr"), 1)

            def stick(l, idx, m0):
                for t in range(NH2 + 2):
                    n = NH2 * idx + t
                    if t < NH2:
                        base = 3 * BANK * (t % 2)
                        if t >= 2:
                            pe.wait_ge(S("k_a"), n - 1)
                        elif t == 0:
                            pe.wait_ge(mix_ready, m0 + 2)
                        for j in (0, 1, 3, 2):
                            e = mm(ps[:, base + ZK[j]:base + ZK[j] + wk(j)], k2[:, t, P * j:P * j + P], q2[:, t, P * j:T],
                                   start=j != 3, stop=True, skip_group_check=True)
                        e.then_inc(S("k_z"), 1)
                    if 1 <= t <= NH2:
                        par, base = (t - 1) % 2, 3 * BANK * ((t - 1) % 2)
                        pe.wait_ge(S("k_ul"), n)
                        for part in (uh[par], ul[par]):
                            for j in range(4):
                                for jj in range(j, 4):
                                    o = base + ZK[j] + P * (jj - j)
                                    e = mm(ps[:, o:o + wk(jj)], negtri[:, :] if jj == j else negones[:, :],
                                           part[:, ZK[jj]:ZK[jj] + wk(jj)], start=False, stop=True, skip_group_check=True)
                        e.then_inc(S("k_cum"), 1)
                    if t >= 2:
                        h = t - 2
                        pe.wait_ge(S("k_a"), n - 1)
                        if h >= 2:
                            pe.wait_ge(mix_ready, m0 + 2 + h - 1)
                        for j in range(4):
                            e = mm(bank(6 + t % 2, T - P * j, P * j), v2[:, j, P * h:P * h + P],
                                   az[h % 2][:, ZK[j]:ZK[j] + wk(j)], start=j == 0, stop=j == 3, skip_group_check=True)
                        e.then_inc(S("k_o"), 1)

            def differential(m0):
                pe.wait_ge(S("d_lam"), 2)
                pe.wait_ge(mix_ready, m0 + 2)
                mm(bank(3, 2), ones[:, :], lam[:, 0:2], start=True, stop=True).then_inc(S("d_lamsum"), 1)

                def scores(hd, c):
                    m = 2 * hd + c
                    for i in (0, 2, 3, 1):
                        o = 3 * BANK * c + ZQ[i]
                        e = mm(ps[:, o:o + wq(i)], q2[:, m, P * i:P * i + P], k2[:, m, 0:wq(i)],
                               start=i != 2, stop=True, skip_group_check=True)
                    e.then_inc(S("d_z"), 1)

                for t in range(4 + 2):
                    if t < 4:
                        if t >= 2:
                            pe.wait_ge(S("d_pt"), t - 1)
                        elif t == 1:
                            pe.wait_ge(S("d_s"), 4)
                        scores(t, 0)
                    if t >= 2:
                        hd = t - 2
                        pe.wait_ge(S("d_pt"), hd + 1)
                        if hd:
                            pe.wait_ge(S("d_on"), 2 * hd)
                        for d in range(2):
                            for j in range(4):
                                e = mm(bank(6 + d, T - P * j, P * j), v2[:, j, 256 * hd + P * d:256 * hd + P * d + P],
                                       dpt[:, ZK[j]:ZK[j] + wk(j)], start=j == 0, stop=j == 3, skip_group_check=True)
                        e.then_inc(S("d_pv"), 1)
                    if 1 <= t <= 4:
                        pe.wait_ge(S("d_p"), 8 * t)
                        for j in (0, 1, 3, 2):
                            for i in range(j, 4):
                                o = ZK[j] + P * (i - j)
                                e = tr(ps[:, o:o + P], dp[2 * (t - 1) % 4][:, ZQ[i] + P * j:ZQ[i] + P * j + P], ident[:, :])
                        e.then_inc(S("d_tr"), 1)
                    if t >= 2:
                        pe.wait_ge(S("d_sq"), 2 * (t - 1))
                        mm(bank(3), ones[:, :], osq[0][:, :], start=True, stop=False)
                        mm(bank(3), ones[:, :], osq[1][:, :], start=False, stop=True).then_inc(S("d_ssum"), 1)
                    if t < 4:
                        if t:
                            pe.wait_ge(S("d_s"), 8 * t)
                        if t >= 2:
                            pe.wait_ge(S("d_sd"), t - 1)
                        else:
                            pe.wait_ge(S("d_lamexp"), 1)
                        scores(t, 1)

            for l in range(NL):
                u0, g0, m0, r = u_layer(l), g_in(l), 8 + 10 * l, 3 + 2 * l
                first_turn(r, u0, 0, 6)
                for n in range(2, L_O):
                    unit_ready(u0 + n)
                    pe.wait_ge(acc_free, g0 + n - 1)
                    if l != 2 and n >= L_V:
                        e = token_tiles((u0 + n) % 2, n % 2, hh, hl)
                    else:
                        e = feature_tiles((u0 + n) % 2, lambda c: bank(2 * (n % 2) + c), XH, XL)[1]
                    e.then_inc(unit_used, 1)
                    memory_step(l, n)
                if l != 2:
                    pe.wait_ge(acc_free, g0 + L_O)
                if l in (0, 3):
                    stick(l, l // 3, m0)
                elif l == 1:
                    differential(m0)
                pe.wait_ge(mix_ready, mix_index(l, 4) + 1)

                def out_proj(half, i):
                    base = 2048 * (1 - half)
                    for j in range(2):
                        if half == 0 and j == 1:
                            pe.wait_ge(mix_ready, m0 + 10)
                        unit_ready(u0 + L_O + 4 * half + j, i, 2)
                        ends = feature_tiles((u0 + L_O + j) % 2, lambda c: ps[:, bass.ds(1024 * i + (base + 512 * c) if isinstance(i, int) else i * 1024 + (base + 512 * c), 512)],
                                             AH, AL, kn=5, k0=5 * j, first=j == 0, last=j == 1, outer_k=False)
                        if j:
                            ends[0].then_inc(resid_done, 1)
                        ends[1].then_inc(unit_used, 1)
                for half in range(2):
                    loop(pe, 2, lambda i: out_proj(half, i), peel=0)
                swiglu(1 + l, u0 + L_GU, g_gu(l), 4 + 2 * l)
            norm_sum(11)
            norm_row(11)
            pe.wait_ge(S("out_scaled"), KD)
            for t in range(TT):
                for d in range(2):
                    n = 2 * t + d
                    if n >= 4:
                        pe.wait_ge(S("out_tile"), n - 3)
                    for f in range(4):
                        e = tr(bank(n % 4, P, P * f), x[:, 4 * d + f, P * t:P * t + P], ident[:, :])
                    e.then_inc(S("out_tr"), 1)


_INS = [
    "x", "norm_mix_g", "w_in", "ssm_lam_re", "ssm_lam_im", "ssm_log_dt", "ssm_b_re", "ssm_b_im",
    "ssm_c_re", "ssm_c_im", "ssm_d", "ssm_w_glu", "ssm_b_glu", "attn_rel_bias", "norm_ssm_out_g",
    "norm_att_out_g", "w_out", "norm_ffn_g", "w_gate", "w_up", "w_down", "norm_final_g", "mem_2",
    "g_mix_2", "w_in_2", "w_mem_kv_2", "w_o_2", "g_ffn_2", "w_ffn_in_2", "w_ffn_out_2",
    "lam_q1_2", "lam_k1_2", "lam_q2_2", "lam_k2_2", "g_diff_head_2", "conv_w_2", "g_mem_2", "g_final_2",
]


def kernel(**inputs):
    import numpy as _np
    import concourse.bacc as _bacc
    from concourse import mybir as _mybir
    from concourse.bass_utils import run_bass_kernel_spmd as _run

    nc = _bacc.Bacc("TRN2", target_bir_lowering=False, num_devices=1, dynamic_dma_scratch_size=1024)
    arrays, aps = {}, {}
    for name in _INS:
        a = _np.ascontiguousarray(inputs[name])
        arrays[f"in_{name}"] = a
        aps[name] = nc.dram_tensor(f"in_{name}", a.shape, _mybir.dt.from_np(a.dtype), kind="ExternalInput").ap()
    out = nc.dram_tensor("out_dram", (T, D), _mybir.dt.float32, kind="ExternalOutput").ap()
    ext_dram = nc.dram_tensor("bias_rows", (NH1, 640), _mybir.dt.float32, kind="Internal").ap()
    build(nc, aps, out, ext_dram)
    r = _run(nc, [arrays], core_ids=[0])
    return r.results[0]["out_dram"].reshape(1, T, D)
```
